# Optimizing a Trainium2 kernel written in Bass

```python
import jax
import jax.numpy as jnp
from jax import lax
import numpy as np

D_MODEL = 2048
BATCH = 1
SEQ = 512
DEPTH = 1
DEC_BATCH = 1
DEC_SEQ = 64
PAST_LEN = 128

CHUNK = 64
N_BRANCH = 3
BRANCH_W = 1024
POOL_WINDOWS = (2, 4, 8, 16)
N_POOL_GROUPS = 4
POOL_GROUP_W = BRANCH_W // N_POOL_GROUPS
POOL_STATE = 15
SB_HEADS = 8
SB_HEAD_DIM = BRANCH_W // SB_HEADS
SB_Q_BLOCK = 128
ML_HEADS = 4
ML_HEAD_DIM = BRANCH_W // ML_HEADS
F_BIAS_INIT = 3.0
RMS_EPS = 1e-6
NEG_BIG = -1e30

OFF_POOL = 0
OFF_SB_Q = OFF_POOL + BRANCH_W
OFF_SB_K = OFF_SB_Q + BRANCH_W
OFF_SB_V = OFF_SB_K + BRANCH_W
OFF_ML_Q = OFF_SB_V + BRANCH_W
OFF_ML_K = OFF_ML_Q + BRANCH_W
OFF_ML_V = OFF_ML_K + BRANCH_W
OFF_ML_O = OFF_ML_V + BRANCH_W
OFF_ML_I = OFF_ML_O + BRANCH_W
OFF_ML_F = OFF_ML_I + ML_HEADS
OFF_Z = OFF_ML_F + ML_HEADS
OFF_GATE = OFF_Z + N_BRANCH * BRANCH_W
IN_COLS = OFF_GATE + N_BRANCH * D_MODEL

kernel_name = "hybrid_pool_stickbreak_mlstm_stream_step"

def rmsnorm(x, g):
    xf = x.astype(jnp.float32)
    xf = xf * lax.rsqrt(jnp.mean(xf * xf, axis=-1, keepdims=True) + RMS_EPS)
    return (xf * g.astype(jnp.float32)).astype(x.dtype)

def pool_mixer(u, prev, pos0, w_pool, scale):
    b, t, c = u.shape
    full = jnp.concatenate([prev.astype(u.dtype), u], axis=1)
    cs = jnp.cumsum(jnp.concatenate([jnp.zeros((b, 1, c), jnp.float32), full.astype(jnp.float32)], axis=1), axis=1)
    pos = pos0 + jnp.arange(t, dtype=jnp.int32)
    base = POOL_STATE + 1
    outs = []
    for gi, w in enumerate(POOL_WINDOWS):
        lo, hi = gi * POOL_GROUP_W, (gi + 1) * POOL_GROUP_W
        wsum = cs[:, base:base + t, lo:hi] - cs[:, base - w:base - w + t, lo:hi]
        cnt = jnp.minimum(pos + 1, w).astype(jnp.float32)[None, :, None]
        pooled = wsum / cnt - u[:, :, lo:hi].astype(jnp.float32)
        outs.append(jnp.einsum('btc,cd->btd', pooled, w_pool[gi].astype(jnp.float32)))
    y = jnp.concatenate(outs, axis=-1) * scale.astype(jnp.float32)
    return y.astype(u.dtype), full[:, -POOL_STATE:]

def stick_breaking(q, k, v, q_pos0):
    b, tq, h, dh = q.shape
    scale = dh ** -0.5
    outs = []
    for start in range(0, tq, SB_Q_BLOCK):
        end = min(start + SB_Q_BLOCK, tq)
        kend = q_pos0 + end
        qb = q[:, start:end].astype(jnp.float32)
        kb = k[:, :kend].astype(jnp.float32)
        vb = v[:, :kend].astype(jnp.float32)
        z = jnp.einsum('bqhd,bkhd->bhqk', qb, kb) * scale
        qpos = q_pos0 + start + jnp.arange(end - start)
        kpos = jnp.arange(kend)
        valid = kpos[None, :] < qpos[:, None]
        log_1m = jnp.where(valid, jax.nn.log_sigmoid(-z), 0.0)
        after = lax.cumsum(log_1m, axis=3, reverse=True) - log_1m
        a = jnp.where(valid, jnp.exp(jax.nn.log_sigmoid(z) + after), 0.0)
        outs.append(jnp.einsum('bhqk,bkhd->bqhd', a, vb))
    return jnp.concatenate(outs, axis=1).astype(q.dtype)

def mlstm_chunkwise(q, k, v, i_pre, log_f, c0, n0, m0):
    b, t, h, dh = q.shape
    nc = -(-t // CHUNK)
    pad = nc * CHUNK - t
    f32 = jnp.float32

    def to_chunks(a, fill):
        a = a.astype(f32)
        a = jnp.pad(a, ((0, 0), (0, pad)) + ((0, 0),) * (a.ndim - 2), constant_values=fill)
        return a.reshape((b, nc, CHUNK) + a.shape[2:])

    qs = jnp.transpose(to_chunks(q, 0.0), (1, 0, 3, 2, 4))
    ks = jnp.transpose(to_chunks(k * (dh ** -0.5), 0.0), (1, 0, 3, 2, 4))
    vs = jnp.transpose(to_chunks(v, 0.0), (1, 0, 3, 2, 4))
    is_ = jnp.transpose(to_chunks(i_pre, NEG_BIG), (1, 0, 3, 2))
    fs = jnp.transpose(to_chunks(log_f, 0.0), (1, 0, 3, 2))
    causal = jnp.tril(jnp.ones((CHUNK, CHUNK), dtype=bool))

    def step(carry, inp):
        c, n, m = carry
        qc, kc, vc, ic, fc = inp
        bcum = jnp.cumsum(fc, axis=-1)
        d = bcum[..., :, None] - bcum[..., None, :] + ic[..., None, :]
        d = jnp.where(causal, d, -jnp.inf)
        g = bcum + m[..., None]
        m_t = jnp.maximum(g, jnp.max(d, axis=-1))
        w_intra = jnp.exp(d - m_t[..., None])
        w_inter = jnp.exp(g - m_t)
        s = jnp.einsum('bhld,bhsd->bhls', qc, kc) * w_intra
        num = jnp.einsum('bhls,bhsv->bhlv', s, vc) + w_inter[..., None] * jnp.einsum('bhlk,bhkv->bhlv', qc, c)
        den = jnp.sum(s, axis=-1) + w_inter * jnp.einsum('bhlk,bhk->bhl', qc, n)
        h_out = num / jnp.maximum(jnp.abs(den), jnp.exp(-m_t))[..., None]
        b_last = bcum[..., -1]
        m_new = m_t[..., -1]
        decay = jnp.exp(b_last + m - m_new)
        w_end = jnp.exp(b_last[..., None] - bcum + ic - m_new[..., None])
        c_new = decay[..., None, None] * c + jnp.einsum('bhs,bhsk,bhsv->bhkv', w_end, kc, vc)
        n_new = decay[..., None] * n + jnp.einsum('bhs,bhsk->bhk', w_end, kc)
        return (c_new, n_new, m_new), h_out

    (c_f, n_f, m_f), hs = lax.scan(step, (c0.astype(f32), n0.astype(f32), m0.astype(f32)), (qs, ks, vs, is_, fs))
    hs = jnp.transpose(hs, (1, 0, 3, 2, 4)).reshape(b, nc * CHUNK, h, dh)[:, :t]
    return hs, c_f, n_f, m_f

def trunk_layer(x, pos0, pool_prev, sb_k_past, sb_v_past, ml_c, ml_n, ml_m,
                g_pre, w_in, b_if, w_pool, pool_scale, ml_hnorm, w_branch, w_out, g_post):
    b, t, _ = x.shape
    f32 = jnp.float32
    xn = rmsnorm(x, g_pre)

    def cols(off, width):
        return jnp.einsum('btd,dc->btc', xn, w_in[:, off:off + width])

    pool_y, pool_new = pool_mixer(cols(OFF_POOL, BRANCH_W), pool_prev, pos0, w_pool, pool_scale)

    q_sb = cols(OFF_SB_Q, BRANCH_W).reshape(b, t, SB_HEADS, SB_HEAD_DIM)
    k_sb = cols(OFF_SB_K, BRANCH_W).reshape(b, t, SB_HEADS, SB_HEAD_DIM)
    v_sb = cols(OFF_SB_V, BRANCH_W).reshape(b, t, SB_HEADS, SB_HEAD_DIM)
    if sb_k_past is None:
        k_all, v_all = k_sb, v_sb
    else:
        k_all = jnp.concatenate([sb_k_past.astype(k_sb.dtype), k_sb], axis=1)
        v_all = jnp.concatenate([sb_v_past.astype(v_sb.dtype), v_sb], axis=1)
    sb_y = stick_breaking(q_sb, k_all, v_all, pos0).reshape(b, t, BRANCH_W)

    q_ml = cols(OFF_ML_Q, BRANCH_W).reshape(b, t, ML_HEADS, ML_HEAD_DIM)
    k_ml = cols(OFF_ML_K, BRANCH_W).reshape(b, t, ML_HEADS, ML_HEAD_DIM)
    v_ml = cols(OFF_ML_V, BRANCH_W).reshape(b, t, ML_HEADS, ML_HEAD_DIM)
    i_pre = cols(OFF_ML_I, ML_HEADS).astype(f32) + b_if[0].astype(f32)
    log_f = jax.nn.log_sigmoid(cols(OFF_ML_F, ML_HEADS).astype(f32) + b_if[1].astype(f32))
    h_ml, c_new, n_new, m_new = mlstm_chunkwise(q_ml, k_ml, v_ml, i_pre, log_f, ml_c, ml_n, ml_m)
    h_ml = h_ml * lax.rsqrt(jnp.mean(h_ml * h_ml, axis=-1, keepdims=True) + RMS_EPS)
    h_ml = h_ml * ml_hnorm.astype(f32).reshape(ML_HEADS, ML_HEAD_DIM)
    ml_y = (h_ml.reshape(b, t, BRANCH_W) * jax.nn.sigmoid(cols(OFF_ML_O, BRANCH_W).astype(f32))).astype(x.dtype)

    merged = None
    for bi, yb in enumerate((pool_y, sb_y, ml_y)):
        gated = yb * jax.nn.silu(cols(OFF_Z + bi * BRANCH_W, BRANCH_W))
        term = jax.nn.sigmoid(cols(OFF_GATE + bi * D_MODEL, D_MODEL)) * jnp.einsum('btw,wd->btd', gated, w_branch[bi])
        merged = term if merged is None else merged + term
    y = jnp.einsum('btd,de->bte', merged, w_out).astype(x.dtype)
    x_out = x + rmsnorm(y, g_post)
    return x_out, pool_new, k_sb, v_sb, c_new, n_new, m_new

def setup_inputs(seed: int = 0) -> dict:
    key = jax.random.key(seed)
    ks = jax.random.split(key, 20)
    nrm = jax.random.normal
    f32 = jnp.float32
    x_prompt = nrm(ks[0], (BATCH, SEQ, D_MODEL), f32)
    x_sample = nrm(ks[1], (DEC_BATCH, DEC_SEQ, D_MODEL), f32)
    cache_sb_k = nrm(ks[2], (DEPTH, DEC_BATCH, PAST_LEN, SB_HEADS, SB_HEAD_DIM), f32)
    cache_sb_v = nrm(ks[3], (DEPTH, DEC_BATCH, PAST_LEN, SB_HEADS, SB_HEAD_DIM), f32)
    state_pool = nrm(ks[4], (DEPTH, DEC_BATCH, POOL_STATE, BRANCH_W), f32)
    state_ml_c = 0.1 * nrm(ks[5], (DEPTH, DEC_BATCH, ML_HEADS, ML_HEAD_DIM, ML_HEAD_DIM), f32)
    state_ml_n = 0.1 * nrm(ks[6], (DEPTH, DEC_BATCH, ML_HEADS, ML_HEAD_DIM), f32)
    state_ml_m = 0.5 * nrm(ks[7], (DEPTH, DEC_BATCH, ML_HEADS), f32)
    g_pre = 1.0 + 0.05 * nrm(ks[8], (DEPTH, D_MODEL), f32)
    w_in = nrm(ks[9], (DEPTH, D_MODEL, IN_COLS), f32) * (D_MODEL ** -0.5)
    b_if = jnp.stack([0.1 * nrm(ks[10], (DEPTH, ML_HEADS), f32),
                      F_BIAS_INIT + 0.1 * nrm(ks[11], (DEPTH, ML_HEADS), f32)], axis=1)
    w_pool = nrm(ks[12], (DEPTH, N_POOL_GROUPS, POOL_GROUP_W, POOL_GROUP_W), f32) * (POOL_GROUP_W ** -0.5)
    pool_scale = 1.0 + 0.1 * nrm(ks[13], (DEPTH, BRANCH_W), f32)
    ml_hnorm = 1.0 + 0.05 * nrm(ks[14], (DEPTH, BRANCH_W), f32)
    w_branch = nrm(ks[15], (DEPTH, N_BRANCH, BRANCH_W, D_MODEL), f32) * (BRANCH_W ** -0.5)
    w_out = nrm(ks[16], (DEPTH, D_MODEL, D_MODEL), f32) * (D_MODEL ** -0.5)
    g_post = 1.0 + 0.05 * nrm(ks[17], (DEPTH, D_MODEL), f32)
    return {"x_prompt": x_prompt, "x_sample": x_sample,
            "cache_sb_k": cache_sb_k, "cache_sb_v": cache_sb_v, "state_pool": state_pool,
            "state_ml_c": state_ml_c, "state_ml_n": state_ml_n, "state_ml_m": state_ml_m,
            "g_pre": g_pre, "w_in": w_in, "b_if": b_if, "w_pool": w_pool, "pool_scale": pool_scale,
            "ml_hnorm": ml_hnorm, "w_branch": w_branch, "w_out": w_out, "g_post": g_post}

def reference(x_prompt, x_sample, cache_sb_k, cache_sb_v, state_pool, state_ml_c, state_ml_n, state_ml_m,
              g_pre, w_in, b_if, w_pool, pool_scale, ml_hnorm, w_branch, w_out, g_post):
    f32 = jnp.float32
    bp = x_prompt.shape[0]
    past_len = cache_sb_k.shape[2]
    xp, xs = x_prompt, x_sample
    pr = [[] for _ in range(6)]
    sa = [[] for _ in range(6)]
    for l in range(DEPTH):
        w = (g_pre[l], w_in[l], b_if[l], w_pool[l], pool_scale[l], ml_hnorm[l], w_branch[l], w_out[l], g_post[l])
        xp, *sp = trunk_layer(xp, 0, jnp.zeros((bp, POOL_STATE, BRANCH_W), xp.dtype), None, None,
                              jnp.zeros((bp, ML_HEADS, ML_HEAD_DIM, ML_HEAD_DIM), f32),
                              jnp.zeros((bp, ML_HEADS, ML_HEAD_DIM), f32),
                              jnp.zeros((bp, ML_HEADS), f32), *w)
        xs, *ss = trunk_layer(xs, past_len, state_pool[l], cache_sb_k[l], cache_sb_v[l],
                              state_ml_c[l], state_ml_n[l], state_ml_m[l], *w)
        for lst, a in zip(pr, sp):
            lst.append(a)
        for lst, a in zip(sa, ss):
            lst.append(a)
    p_pool, p_k, p_v, p_c, p_n, p_m = [jnp.stack(a, axis=0) for a in pr]
    s_pool, s_k, s_v, s_c, s_n, s_m = [jnp.stack(a, axis=0) for a in sa]
    return (xp, xs, p_k, p_v, p_pool, p_c, p_n, p_m, s_k, s_v, s_pool, s_c, s_n, s_m)


_drawn_inputs = setup_inputs


def setup_inputs(seed=0):
    import zlib

    import numpy as np

    out = dict(_drawn_inputs(seed))
    spreads = {}
    factors = {'cache_sb_k': 2.772, 'state_ml_n': 48.375, 'state_ml_m': 3.163, 'ml_hnorm': 3.575}
    for name, (base, spread) in spreads.items():
        noise = np.random.default_rng([zlib.crc32(name.encode()), seed]).standard_normal(out[name].shape)
        drawn = base * np.exp(spread * noise) if base else spread * noise
        out[name] = jnp.asarray(drawn.astype(out[name].dtype))
    for name, factor in factors.items():
        out[name] = (out[name] * factor).astype(out[name].dtype)
    return out
```

```python
import concourse.bass as bass
from concourse import mybir
from contextlib import ExitStack

F32 = mybir.dt.float32
F32R = mybir.dt.float32r
ALU = mybir.AluOpType
ACT = mybir.ActivationFunctionType
AXX = mybir.AxisListType.X

P = 128
D = 2048
KD = D // P
W = 1024
KW = W // P
TP, TS = 512, 64
T = TP + TS
TH = T // 2
PAST = 128
SBH, DH = 8, 128
MLH, MDH = 4, 256
MC = MDH // P
PG = 4
WINDOWS = (2, 4, 8, 16)
PST = 15
EPS = 1e-6
NBR = 3
OFF_POOL, OFF_SQ, OFF_SK, OFF_SV = 0, W, 2 * W, 3 * W
OFF_MQ, OFF_MK, OFF_MV, OFF_MO, OFF_MI = 4 * W, 5 * W, 6 * W, 7 * W, 8 * W
OFF_Z = OFF_MI + 2 * MLH
OFF_G = OFF_Z + NBR * W
NT = TP // P
NB = NT + 1
UW = 2 * (PST + 1) + T

HK = 8
RAW, RING = 2, 4

POOL_IT, POOL_HALVES, POOL_TILES = PG, 8, 4
SB_IT, SB_HALVES, SB_TILES = SBH, 8, 4
ML_IT, ML_HALVES, ML_TILES = MLH, 20, 10
MG_IT, MG_HALVES, MG_TILES = NBR * 4, 12, 8
OUT_IT, OUT_HALVES, OUT_TILES = KD // 2, 4, 2
H_POOL, T_POOL = 2, 1
H_SB, T_SB = H_POOL + POOL_IT * POOL_HALVES, T_POOL + POOL_IT * POOL_TILES
H_ML, T_ML = H_SB + SB_IT * SB_HALVES, T_SB + SB_IT * SB_TILES
H_MG, T_MG = H_ML + ML_IT * ML_HALVES, T_ML + ML_IT * ML_TILES
H_OUT, T_OUT = H_MG + MG_IT * MG_HALVES, T_MG + MG_IT * MG_TILES

SB_BLOCKS = [(0, 0, 512, 0), (1, 512, 384, 128), (3, 896, 128, 384), (2, 1024, 256, 256),
             ("past", 1280, 64, TP), (4, 1344, 64, TP)]
SB_W = 1408
ML_BLOCKS = [(0, 0, 512, 0), (1, 512, 384, 128), (3, 896, 128, 384), (2, 1024, 256, 256),
             (4, 1280, 64, TP)]
ML_W = 1344
TOKEN0 = [0, 128, 256, 384, T - P]


EM_MAX = 45.0
DEN_MIN = 1e-14
VECTORS = 5


class At:

    def __init__(self, base, i=0, per=0):
        self.base, self.i, self.per = base, i, per

    def __add__(self, n):
        return At(self.base + n, self.i, self.per)

    def value(self, plus=0):
        return self.i * self.per + (self.base + plus)

    def count(self, slots):
        assert self.per % slots == 0
        return self.i * (self.per // slots) + (self.base // slots + 1)


class Steps:

    def __init__(self, eng, sem):
        self.eng, self.sem, self.base, self.i, self.per, self.k = eng, sem, 0, 0, 0, 0

    def begin(self, i, per):
        self.i, self.per, self.k = i, per, 0

    def end(self, times):
        assert self.k == self.per, (self.k, self.per)
        self.base += self.per * times

    def link(self, ins):
        self.k += 1
        ins.then_inc(self.sem, 1)
        self.eng.wait_ge(self.sem, self.i * self.per + (self.base + self.k))


def hybrid_layer(nc, x_prompt, x_sample, cache_sb_k, cache_sb_v, state_pool, state_ml_c, state_ml_n,
                 state_ml_m, g_pre, w_in, b_if, w_pool, pool_scale, ml_hnorm, w_branch, w_out, g_post,
                 y_prompt, y_sample, p_k, p_v, p_pool, p_c, p_n, p_m, s_k, s_v, s_pool, s_c, s_n, s_m):
    w_in_v = w_in.rearrange("a (k p) c -> p (a k) c", p=P)
    w_br_v = w_branch.rearrange("a b (k p) c -> p (a b) k c", p=P)
    w_out_v = w_out.rearrange("a (k p) c -> p (a k) c", p=P)
    w_pool_v = w_pool.rearrange("a g (k p) c -> p (a g) k c", p=P)
    c0_v = state_ml_c.rearrange("a b h (k p) v -> p (a b h) k v", p=P)
    n0_v = state_ml_n.rearrange("a b h (k p) -> p (a b h k)", p=P)
    p_c_v = p_c.rearrange("a b h (k p) v -> p (a b h) k v", p=P)
    s_c_v = s_c.rearrange("a b h (k p) v -> p (a b h) k v", p=P)
    p_n_v = p_n.rearrange("a b h (k p) -> p (a b h k)", p=P)
    s_n_v = s_n.rearrange("a b h (k p) -> p (a b h k)", p=P)
    xp_v = x_prompt.rearrange("a (m p) d -> p (a m) d", p=P)
    yp_v = y_prompt.rearrange("a (m p) d -> p (a m) d", p=P)
    pk_v = p_k.rearrange("a b (m p) h d -> p (a b m) (h d)", p=P)
    pv_v = p_v.rearrange("a b (m p) h d -> p (a b m) (h d)", p=P)
    sk_v = s_k.rearrange("a b t h d -> (a b t) (h d)")
    sv_v = s_v.rearrange("a b t h d -> (a b t) (h d)")
    past_k_v = cache_sb_k.rearrange("a b t h d -> (a b t) (h d)")
    past_v_v = cache_sb_v.rearrange("a b t h d -> (a b t) (h d)")
    p_pool_v = p_pool.rearrange("a b t c -> (a b t) c")
    s_pool_v = s_pool.rearrange("a b t c -> (a b t) c")
    gated_dram = nc.dram_tensor("gated_scratch", (2 * NBR * KW * P, T), F32R, kind="Internal").ap()
    gated_v = gated_dram.rearrange("(s k p) t -> p s k t", s=2, p=P)

    ctx = ExitStack()
    with ctx:
        def sb(name, shape, dt=F32, where=ctx):
            return where.enter_context(nc.sbuf_tensor(name, shape, dt))

        def sem(name):
            return ctx.enter_context(nc.semaphore(name))

        x_hi = sb("x_hi", [P, KD, T], F32R)
        x_lo = sb("x_lo", [P, KD, T], F32R)
        raw = sb("raw", [P, RAW, HK, P])
        w_hi = sb("w_hi", [P, RING, HK, P], F32R)
        w_lo = sb("w_lo", [P, RING, HK, P], F32R)
        ident = sb("ident", [P, P])
        ones = sb("ones", [P, P])
        negones = sb("negones", [P, P])
        negtri = sb("negtri", [P, P])
        small = sb("small", [P, 24])
        hnorm = sb("hnorm", [P, KW])
        pscale = sb("pscale", [P, KW])

        with ExitStack() as e:
            xt = sb("xt", [P, NB, D], where=e)
            gpre_b = sb("gpre_b", [P, D], where=e)
            junk = sb("junk", [P, D], where=e)
        with ExitStack() as e:
            if_rows = sb("if_rows", [2 * MLH, T], where=e)
            sig = sb("sig", [P, T], where=e)
            silu = sb("silu", [P, 2, T], where=e)
            gated = sb("gated", [P, T], where=e)
            g_hi = sb("g_hi", [P, T], F32R, where=e)
            g_lo = sb("g_lo", [P, T], F32R, where=e)
            with ExitStack() as e2:
                U = sb("U", [P, 2, UW], where=e2)
                sums = sb("sums", [P, 2, UW], where=e2)
                pooled = sb("pooled", [P, 2, T], where=e2)
                first = sb("first", [P, PST + 1], where=e2)
                inv_cnt = sb("inv_cnt", [P, PST + 1], where=e2)
                wp = sb("wp", [P, 1, 2, 2 * P], where=e2)
                spool = sb("spool", [PST, W], where=e2)
                pool_row = sb("pool_row", [PST, 4 * P], where=e2)
                state_row = sb("state_row", [P, KW, PST + 1], where=e2)
            mask = sb("mask", [P, SB_W], where=e)
            XA = sb("XA", [P, SB_W], where=e)
            XB = sb("XB", [P, SB_W], where=e)
            qT = sb("qT", [P, MC, T], where=e)
            kT = sb("kT", [P, MC, T], where=e)
            vT = sb("vT", [P, MC, T], where=e)
            with ExitStack() as e2:
                XC = sb("XC", [P, SB_W], where=e2)
                k_tok = sb("k_tok", [P, (NB + 1) * P], where=e2)
                v_tok = sb("v_tok", [P, NB * P], where=e2)
                past_k = sb("past_k", [P, P], where=e2)
                past_v = sb("past_v", [P, P], where=e2)
            with ExitStack() as e2:
                NG = sb("NG", [P, MLH, T], where=e2)
                EM = sb("EM", [P, MLH, T], where=e2)
                mk_tok = sb("mk_tok", [P, NB, MDH], where=e2)
                mv_tok = sb("mv_tok", [P, NB, MDH + 1], where=e2)
                c0 = sb("c0", [P, MC, MDH], where=e2)
                og = sb("og", [P, MC, T], where=e2)
                num = sb("num", [P, MC, T], where=e2)
                den = sb("den", [P, T], where=e2)
                qw = sb("qw", [P, MC, TS], where=e2)
                n0b = sb("n0b", [P, MC, P], where=e2)
                wi = sb("wi", [P, MLH, TS], where=e2)
                acol = sb("acol", [P, NB, MLH], where=e2)
                wend = sb("wend", [P, MLH, NB], where=e2)
                m0b = sb("m0b", [P, MLH], where=e2)
                decay = sb("decay", [P, MLH], where=e2)
                n0 = sb("n0", [P, MLH * MC], where=e2)
                n_out = sb("n_out", [P, 2, MLH * MC], where=e2)
        with ExitStack() as e:
            gt_hi = sb("gt_hi", [P, KW, T], F32R, where=e)
            gt_lo = sb("gt_lo", [P, KW, T], F32R, where=e)
            merged = sb("merged", [P, KD, T], where=e)
            gsig = sb("gsig", [P, T], where=e)
            term = sb("term", [P, T], where=e)
        with ExitStack() as e:
            x_again = sb("x_again", [P, NB, D], where=e)
            y_tok = sb("y_tok", [P, NB, D], where=e)
            gpost_b = sb("gpost_b", [P, D], where=e)
            yT = sb("yT", [P, T], where=e)
            ysq = sb("ysq", [P, NB, P], where=e)
            ysums = sb("ysums", [P, NB, KD], where=e)

        ROWS = 2 * MLH
        softp, lf = kT[0:ROWS, 0, :], kT[0:ROWS, 1, :]
        fsel, fcum = qT[0:MLH, 0, :], qT[0:MLH, 1, :]
        arow, grow = vT[0:MLH, 0, :], vT[0:MLH, 1, :]
        frow, onesrow = XA[0:MLH, 0:T], XA[0:MLH, T:2 * T]
        negsel = XB[0:MLH, 0:MLH * P].rearrange("p (h j) -> p h j", h=MLH)
        selF = XB[0:ROWS, MLH * P:MLH * P + MLH]
        ss_x, rs_x = small[:, 0:NB], small[:, NB:2 * NB]
        ss_y, rs_y = small[:, 10:10 + NB], small[:, 15:15 + NB]
        bif, m0row = small[0:ROWS, 20:21], small[0:MLH, 21:22]

        pp = ctx.enter_context(nc.psum_tensor("pp", [P, 4, 512], F32))
        M = ctx.enter_context(nc.psum_tensor("M", [P, 4 * 512], F32))

        def pair(t):
            return pp[:, 2 * (t.base % 2):2 * (t.base % 2) + 2, 0:TH]

        def two(ap):
            return ap.rearrange("p (b t) -> p b t", b=2)

        def evacuated(eng, t):
            eng.wait_ge(psum_free[t.base % 2], t.count(2))

        w_loaded = [sem(f"w_loaded{r}") for r in range(RAW)]
        w_hi_ready, w_lo_ready, w_used = sem("w_hi_ready"), sem("w_lo_ready"), sem("w_used")
        psum_free = [sem("psum_free0"), sem("psum_free1")]
        dve_steps, act_steps, pool_steps = sem("dve_steps"), sem("act_steps"), sem("pool_steps")
        x_loaded = [sem(f"x_loaded{m}") for m in range(NB)]
        vectors_loaded, consts_ready, small_cleared = sem("vectors_loaded"), sem("consts_ready"), sem("small_cleared")
        sq_done, ms_ready, root_x_ready = sem("sq_done"), sem("ms_ready"), sem("root_x_ready")
        xs_ready, xtr_done, xhi_done, xlo_done = sem("xs_ready"), sem("xtr_done"), sem("xhi_done"), sem("xlo_done")
        pool_turns, states_out = sem("pool_turns"), sem("states_out")
        sig_ready, dabs_ready = sem("sig_ready"), sem("dabs_ready")
        g_ready, ghi_ready, glo_ready, g_stored = sem("g_ready"), sem("ghi_ready"), sem("glo_ready"), sem("g_stored")
        spool_loaded, sptr_done, sptr_copied = sem("spool_loaded"), sem("sptr_done"), sem("sptr_copied")
        wp_loaded, pooled_ready, wpool_done = sem("wp_loaded"), sem("pooled_ready"), sem("wpool_done")
        urow_done, urow_copied, urow_stored = sem("urow_done"), sem("urow_copied"), sem("urow_stored")
        past_k_loaded, past_v_loaded = sem("past_k_loaded"), sem("past_v_loaded")
        ktr_done, ktok_ready, k_stored = sem("ktr_done"), sem("ktok_ready"), sem("k_stored")
        z_done, zs_ready, soft_ready = sem("z_done"), sem("zs_ready"), sem("soft_ready")
        L_ready, Lm_ready, after_done = sem("L_ready"), sem("Lm_ready"), sem("after_done")
        vtok_ready, v_stored, s_ready = sem("vtok_ready"), sem("v_stored"), sem("s_ready")
        a_ready, am_ready, av_done = sem("a_ready"), sem("am_ready"), sem("av_done")
        gate_dve, gate_act, gate_pe, sel_ready = sem("gate_dve"), sem("gate_act"), sem("gate_pe"), sem("sel_ready")
        gate_loads, m_stored, m_out = sem("gate_loads"), sem("m_stored"), sem("m_out")
        c0_loaded, mktr_done, mktok_ready, kw_ready = sem("c0_loaded"), sem("mktr_done"), sem("mktok_ready"), sem("kw_ready")
        D_ready, W_ready, Wm_ready = sem("D_ready"), sem("W_ready"), sem("Wm_ready")
        scores_done, sw_ready, mvtr_done, mvtok_ready = sem("scores_done"), sem("sw_ready"), sem("mvtr_done"), sem("mvtok_ready")
        num_done, num_ready, squares_ready = sem("num_done"), sem("num_ready"), sem("squares_ready")
        dmax_ready, dsq_ready, ssq_done, ssq_read, root_ready = sem("dmax_ready"), sem("dsq_ready"), sem("ssq_done"), sem("ssq_read"), sem("root_ready")
        state_done, state_ready, state_stored, n_stored = sem("state_done"), sem("state_ready"), sem("state_stored"), sem("n_stored")
        gt_loaded, merged_zero, branch_done = sem("gt_loaded"), sem("merged_zero"), sem("branch_done")
        mhi_ready, mlo_ready, late_loads = sem("mhi_ready"), sem("mlo_ready"), sem("late_loads")
        ytr_done, yg_ready, ysq_done = sem("ytr_done"), sem("yg_ready"), sem("ysq_done")
        yms_ready, root_y_ready, yout_ready, y_stored = sem("yms_ready"), sem("root_y_ready"), sem("yout_ready"), sem("y_stored")

        block = ctx.enter_context(nc.Block())

        @block.sync
        def _(sp):
            def load(n, src):
                if n.base >= RAW:
                    sp.wait_ge(w_lo_ready, n.value(1 - RAW))
                slot = n.base % RAW
                sp.dma_start(raw[:, slot, :, :], src).then_inc(w_loaded[slot], 16)

            def load_tile(n, col):
                load(n, w_in_v[:, 0:HK, bass.ds(col, P)])
                load(n + 1, w_in_v[:, HK:2 * HK, bass.ds(col, P)])

            load_tile(At(0), OFF_MI)
            with sp.Fori(0, POOL_IT) as g:
                n = At(H_POOL, g, POOL_HALVES)
                for c, off in enumerate([OFF_POOL, OFF_POOL + P, OFF_Z, OFF_Z + P]):
                    load_tile(n + 2 * c, g * (2 * P) + off)
            with sp.Fori(0, SB_IT) as h:
                n = At(H_SB, h, SB_HALVES)
                for c, off in enumerate([OFF_SK, OFF_SQ, OFF_SV, OFF_Z + W]):
                    load_tile(n + 2 * c, h * P + off)
            with sp.Fori(0, ML_IT) as h:
                n = At(H_ML, h, ML_HALVES)
                for c, off in enumerate([OFF_MQ, OFF_MK, OFF_MV, OFF_MO, OFF_Z + 2 * W]):
                    for j in range(MC):
                        load_tile(n + (2 * MC * c + 2 * j), h * MDH + (off + j * P))
            with sp.Fori(0, NBR) as b:
                with sp.Fori(0, 4) as dd:
                    n = At(H_MG, b * 4 + dd, MG_HALVES)
                    for j in range(4):
                        load_tile(n + 3 * j, b * D + dd * (4 * P) + (OFF_G + j * P))
                        load(n + (3 * j + 2), w_br_v[:, b, :, bass.ds(dd * (4 * P) + j * P, P)])
            with sp.Fori(0, OUT_IT) as d:
                n = At(H_OUT, d, OUT_HALVES)
                for j in range(2):
                    for s in range(2):
                        load(n + (2 * j + s), w_out_v[:, s * HK:(s + 1) * HK, bass.ds(d * (2 * P) + j * P, P)])
            for m in range(NB):
                sp.wait_ge(yout_ready, m + 1)
                if m < NT:
                    sp.dma_start(yp_v[:, m, :], y_tok[:, m, :]).then_inc(y_stored, 16)
                else:
                    sp.dma_start(y_sample[0, :, :], y_tok[0:TS, m, :]).then_inc(y_stored, 16)
            sp.wait_ge(y_stored, 16 * NB)

        @block.tensor
        def _(pe):
            def half(n, t, xh, xl, k0, opens, closes):
                pe.wait_ge(w_lo_ready, n.value(1))
                if opens and t.base >= 2:
                    evacuated(pe, t + (-2))
                slot, out = n.base % RING, pair(t)
                for k in range(HK):
                    for s, (ws, xs) in enumerate(((w_hi, xh), (w_hi, xl), (w_lo, xh))):
                        for b in range(2):
                            i = nc.tensor.matmul(
                                out[:, b, :], ws[:, slot, k, :], xs[:, k0 + k, b * TH:(b + 1) * TH],
                                start=opens and k == 0 and s == 0, stop=closes and k == HK - 1 and s == 2)
                i.then_inc(w_used, 1)

            def tile(n, t):
                half(n, t, x_hi, x_lo, 0, True, False)
                half(n + 1, t, x_hi, x_lo, HK, False, True)

            def transposes(blocks):
                for out, src in blocks:
                    k = src.shape[0]
                    i = nc.tensor.transpose(out, src, ident[0:k, 0:k])
                return i

            pe.sem_inc(wpool_done, 1)
            pe.wait_ge(consts_ready, 4)
            for m in range(NB):
                rows = P if m < NT else TS
                pe.wait_ge(xs_ready, m + 1)
                for q in range(4):
                    if m:
                        pe.wait_ge(xlo_done, 4 * m + q - 3)
                    transposes([(M[:, 512 * q + P * j:512 * q + P * j + rows],
                                 xt[0:rows, m, (4 * q + j) * P:(4 * q + j + 1) * P]) for j in range(4)]
                               ).then_inc(xtr_done, 1)
            pe.wait_ge(xlo_done, 4 * NB)
            tile(At(0), At(0))
            pe.wait_ge(spool_loaded, 16)
            transposes([(M[:, 16 * j:16 * j + PST], spool[0:PST, j * P:(j + 1) * P]) for j in range(KW)]
                       ).then_inc(sptr_done, 1)
            pe.wait_ge(sptr_copied, 1)
            with pe.Fori(0, POOL_IT) as g:
                n, t = At(H_POOL, g, POOL_HALVES), At(T_POOL, g, POOL_TILES)
                tile(n, t)
                tile(n + 2, t + 1)
                tile(n + 4, t + 2)
                pe.wait_ge(pooled_ready, g * 2 + 2)
                pe.wait_ge(wp_loaded, g * 16 + 16)
                pe.wait_ge(urow_copied, g + 1)
                for c in range(2):
                    for b in range(2):
                        for k in range(2):
                            i = nc.tensor.matmul(M[:, 1024 * c + 512 * b:1024 * c + 512 * b + TH],
                                                 wp[:, 0, k, c * P:(c + 1) * P],
                                                 pooled[:, k, b * TH:(b + 1) * TH], start=k == 0, stop=k == 1)
                i.then_inc(wpool_done, 1)
                tile(n + 6, t + 3)
                pe.wait_ge(g_ready, g * 2 + 2)
                transposes([(M[0:PST, (2 * c + s) * P:(2 * c + s + 1) * P], U[:, c, o:o + PST])
                            for c in range(2) for s, o in enumerate((1 + TP, UW - PST))]).then_inc(urow_done, 1)

            def weigh_values(prev):
                pe.wait_ge(am_ready, prev + 1)
                pe.wait_ge(vtok_ready, prev + 1)
                pe.wait_ge(past_v_loaded, prev * 16 + 16)
                for s, (kb, col, w, q0) in enumerate(SB_BLOCKS[:4]):
                    nc.tensor.matmul(M[:, 1536 + q0:1536 + q0 + w], v_tok[:, (kb + 1) * P:(kb + 2) * P],
                                     XB[:, col:col + w], start=s == 0, stop=s == 3)
                nc.tensor.matmul(M[:, 1024:1024 + TS], past_v[:, :], XB[:, 1280:1344], start=True, stop=False)
                nc.tensor.matmul(M[:, 1024:1024 + TS], v_tok[:, 0:P], XB[:, 1344:1408], start=False, stop=True
                                 ).then_inc(av_done, 1)

            pe.wait_ge(urow_copied, POOL_IT + 1)

            def head(i, is_first):
                n, t = At(H_SB, i, SB_HALVES), At(T_SB, i, SB_TILES)
                tile(n, t)
                if not is_first:
                    weigh_values(i - 1)
                tile(n + 2, t + 1)
                evacuated(pe, t)
                pe.wait_ge(past_k_loaded, i * 16 + 16)
                if not is_first:
                    pe.wait_ge(s_ready, i * 1)
                transposes([(M[:, j * P:(j + 1) * P], kT[:, 0, TOKEN0[j]:TOKEN0[j] + P]) for j in range(NB)]
                           + [(M[:, NB * P:(NB + 1) * P], past_k[:, :])]).then_inc(ktr_done, 1)
                tile(n + 4, t + 2)
                evacuated(pe, t + 1)
                pe.wait_ge(ktok_ready, i + 1)
                pe.wait_ge(g_ready, i + 8)
                for kb, col, w, q0 in SB_BLOCKS:
                    keys = k_tok[:, NB * P:(NB + 1) * P] if kb == "past" else kT[:, 0, TOKEN0[kb]:TOKEN0[kb] + P]
                    m = nc.tensor.matmul(M[:, col:col + w], keys, qT[:, 0, q0:q0 + w], start=True, stop=True)
                m.then_inc(z_done, 1)
                tile(n + 6, t + 3)
                pe.wait_ge(Lm_ready, i + 1)
                evacuated(pe, t + 2)
                at = {kb: (col, w, q0) for kb, col, w, q0 in SB_BLOCKS}
                for kb, col, w, q0 in SB_BLOCKS:
                    later = [4] if kb == "past" else [x for x in range(NT) if kb < x] if kb < NT else []
                    nc.tensor.matmul(M[:, col:col + w], negtri[:, :], XC[:, col:col + w], start=True, stop=not later)
                    for x in later:
                        c2, w2, q2 = at[x]
                        nc.tensor.matmul(M[:, col + q2 - q0:col + q2 - q0 + w2], negones[:, :], XC[:, c2:c2 + w2],
                                         start=False, stop=x == later[-1])
                transposes([(M[:, SB_W:SB_W + P], vT[:, 0, TOKEN0[4]:TOKEN0[4] + P])]
                           + [(M[:, 1536 + j * P:1536 + (j + 1) * P], vT[:, 0, TOKEN0[j]:TOKEN0[j] + P])
                              for j in range(NT)]).then_inc(after_done, 1)

            head(0, True)
            with pe.Fori(1, SB_IT) as i:
                head(i, False)
            weigh_values(SB_IT - 1)

            pe.wait_ge(g_ready, 16)
            pe.wait_ge(s_ready, SB_IT)
            pe.wait_ge(sel_ready, 2)
            pe.wait_ge(gate_dve, 1)
            for b in range(2):
                m = nc.tensor.matmul(M[0:MLH, 512 * b:512 * b + TH], selF, lf[:, b * TH:(b + 1) * TH], start=True, stop=True)
            m.then_inc(gate_pe, 1)
            pe.wait_ge(gate_dve, 2)
            transposes([(M[:, 1024 + MLH * j:1024 + MLH * (j + 1)], arow[:, TOKEN0[j]:TOKEN0[j] + P]) for j in range(NB)]
                       ).then_inc(gate_pe, 1)
            for h in range(MLH):
                for r, row in enumerate((grow, frow)):
                    s = 2 * h + r
                    if s:
                        pe.wait_ge(gate_dve, 3 if s == 1 else s + 2)
                    for b in range(2):
                        m = nc.tensor.matmul(M[:, 1024 * r + 512 * b:1024 * r + 512 * b + TH],
                                             negsel[:, h, :], row[:, b * TH:(b + 1) * TH], start=True, stop=True)
                    m.then_inc(gate_pe, 1)
            pe.wait_ge(gate_dve, 3 + 2 * MLH)

            with pe.Fori(0, ML_IT) as i:
                n, t = At(H_ML, i, ML_HALVES), At(T_ML, i, ML_TILES)
                for c in range(5):
                    tile(n + 2 * c, t + c)
                evacuated(pe, t + 3)
                evacuated(pe, t + 2)
                pe.wait_ge(state_ready, i + 1)
                transposes([(M[:, MDH * j + P * c:MDH * j + P * (c + 1)], kT[:, c, TOKEN0[j]:TOKEN0[j] + P])
                            for j in range(NB) for c in range(MC)]).then_inc(mktr_done, 1)
                tile(n + 10, t + 5)
                pe.wait_ge(mktok_ready, i + 1)
                for kb, col, w, q0 in ML_BLOCKS:
                    for c in range(MC):
                        m = nc.tensor.matmul(M[:, col:col + w], kT[:, c, TOKEN0[kb]:TOKEN0[kb] + P],
                                             qT[:, c, q0:q0 + w], start=c == 0, stop=c == MC - 1)
                m.then_inc(scores_done, 1)
                tile(n + 12, t + 6)
                evacuated(pe, t + 4)
                evacuated(pe, t + 5)
                pe.wait_ge(sw_ready, i + 1)
                transposes([(M[:, MDH * j + P * c:MDH * j + P * (c + 1)], vT[:, c, TOKEN0[j]:TOKEN0[j] + P])
                            for j in range(NB) for c in range(MC)]).then_inc(mvtr_done, 1)
                tile(n + 14, t + 7)
                pe.wait_ge(mvtok_ready, i + 1)
                pe.wait_ge(c0_loaded, i * 16 + 16)
                for v in range(3):
                    for s, (kb, col, w, q0) in enumerate(ML_BLOCKS[:4]):
                        lhs = ones[:, :] if v == 2 else mv_tok[:, kb, v * P:(v + 1) * P]
                        nc.tensor.matmul(M[:, 512 * v + q0:512 * v + q0 + w], lhs, XB[:, col:col + w],
                                         start=s == 0, stop=s == 3)
                for v in range(3):
                    lhs = ones[:, :] if v == 2 else mv_tok[:, 4, v * P:(v + 1) * P]
                    out = M[:, 1536 + TS * v:1536 + TS * (v + 1)]
                    nc.tensor.matmul(out, lhs, XB[:, 1280:1344], start=True, stop=False)
                    for c in range(MC):
                        lhs = n0b[:, c, :] if v == 2 else c0[:, c, v * P:(v + 1) * P]
                        m = nc.tensor.matmul(out, lhs, qw[:, c, :], start=False, stop=c == MC - 1)
                m.then_inc(num_done, 1)
                tile(n + 16, t + 8)
                pe.wait_ge(squares_ready, i + 1)
                for b in range(2):
                    for c in range(MC):
                        m = nc.tensor.matmul(M[:, 512 * b:512 * b + TH], ones[:, :],
                                             XA[:, c * T + b * TH:c * T + (b + 1) * TH], start=c == 0, stop=c == MC - 1)
                m.then_inc(ssq_done, 1)
                tile(n + 18, t + 9)
                pe.wait_ge(kw_ready, i + 1)
                pe.wait_ge(ssq_read, i + 1)
                for c in range(MC):
                    for kb in range(NT):
                        nc.tensor.matmul(M[:, 512 * c:512 * c + MDH + 1], mk_tok[:, kb, c * P:(c + 1) * P],
                                         mv_tok[:, kb, :], start=kb == 0, stop=kb == NT - 1)
                    m = nc.tensor.matmul(M[:, 1024 + 512 * c:1024 + 512 * c + MDH + 1], mk_tok[:, NT, c * P:(c + 1) * P],
                                         mv_tok[:, NT, :], start=True, stop=True)
                m.then_inc(state_done, 1)

            with pe.Fori(0, NBR) as b:
                with pe.Fori(0, 4) as dd:
                    it = b * 4 + dd
                    n, t = At(H_MG, it, MG_HALVES), At(T_MG, it, MG_TILES)
                    for j in range(4):
                        tile(n + 3 * j, t + 2 * j)
                        if j == 0:
                            pe.wait_ge(gt_loaded, b * 32 + 32)
                        half(n + (3 * j + 2), t + (2 * j + 1), gt_hi, gt_lo, 0, True, True)

            def out_tiles(d, is_first):
                n, t = At(H_OUT, d, OUT_HALVES), At(T_OUT, d, OUT_TILES)
                nr = At(0, d, OUT_TILES)
                for j in range(2):
                    if is_first and j == 0:
                        for s in range(2):
                            pe.wait_ge(mlo_ready, HK * (s + 1))
                            half(n + s, t, x_hi, x_lo, s * HK, s == 0, s == 1)
                    else:
                        tile(n + 2 * j, t + j)
                    evacuated(pe, t + j)
                    if not is_first:
                        pe.wait_ge(ysq_done, (nr + j).value(-1))
                    transposes([(M[:, 1024 * j + P * m:1024 * j + P * (m + 1)], yT[:, m * P:(m + 1) * P]) for m in range(NT)]
                               + [(M[0:TS, 1024 * j + 512:1024 * j + 640], yT[:, TP:T])]).then_inc(ytr_done, 1)

            pe.wait_ge(state_ready, MLH + 1)
            out_tiles(0, True)
            with pe.Fori(1, OUT_IT) as d:
                out_tiles(d, False)

        @block.scalar
        def _(act):
            steps = Steps(act, act_steps)

            def split_hi(n):
                act.wait_ge(w_loaded[n.base % RAW], n.count(RAW) * 16)
                if n.base >= RING:
                    act.wait_ge(w_used, n.value(1 - RING))
                nc.scalar.activation(w_hi[:, n.base % RING, :, :], raw[:, n.base % RAW, :, :], ACT.Copy
                                     ).then_inc(w_hi_ready, 1)

            def split2(n):
                split_hi(n)
                split_hi(n + 1)

            def sigmoid_for_dve(n_last, t):
                act.wait_ge(w_used, n_last.value(1))
                nc.scalar.activation(two(sig[:, :]), pair(t), ACT.Sigmoid).then_inc(sig_ready, 1)

            def gated_hi(k):
                act.wait_ge(g_ready, k)
                if not (isinstance(k, int) and k == 1):
                    act.wait_ge(g_stored, (k - 1) * 32)
                nc.scalar.activation(g_hi[:, :], gated[:, :], ACT.Copy).then_inc(ghi_ready, 1)

            act.wait_ge(small_cleared, 1)
            for m in range(NB):
                rows = P if m < NT else TS
                act.wait_ge(x_loaded[m], 16)
                if m:
                    act.wait_ge(sq_done, m)
                nc.scalar.activation(junk[0:rows, :], xt[0:rows, m, :], ACT.Square,
                                     accum_out=ss_x[0:rows, m:m + 1]).then_inc(sq_done, 1)
            act.wait_ge(ms_ready, 1)
            nc.scalar.activation(rs_x, ss_x, ACT.Sqrt).then_inc(root_x_ready, 1)
            split2(At(0))
            for m in range(NB):
                rows = P if m < NT else TS
                for q in range(4):
                    act.wait_ge(xtr_done, 4 * m + q + 1)
                    nc.scalar.activation(x_hi[:, 4 * q:4 * q + 4, m * P:m * P + rows],
                                         M[:, 512 * q:512 * (q + 1)].rearrange("p (j r) -> p j r", j=4)[:, :, 0:rows],
                                         ACT.Copy).then_inc(xhi_done, 1)
            split2(At(2))
            def group(g):
                n, t = At(H_POOL, g, POOL_HALVES), At(T_POOL, g, POOL_TILES)
                split2(n + 2)
                split2(n + 4)
                split2(n + 6)
                evacuated(act, t + (-1))
                sigmoid_for_dve(n + 5, t + 2)
                gated_hi(g * 2 + 1)
                split2(n + 8)
                evacuated(act, t + 2)
                sigmoid_for_dve(n + 7, t + 3)
                gated_hi(g * 2 + 2)

            group(0)
            with act.Fori(1, POOL_IT) as g:
                group(g)

            steps.begin(0, 2)

            def head(i, is_first):
                n, t = At(H_SB, i, SB_HALVES), At(T_SB, i, SB_TILES)
                steps.begin(i, 2)
                split2(n + 2)
                if not is_first:
                    gated_hi(i + 8)
                split2(n + 4)
                split2(n + 6)
                act.wait_ge(zs_ready, i + 1)
                steps.link(nc.scalar.activation(XB[:, :], XA[:, :], ACT.Abs))
                steps.link(nc.scalar.activation(XB[:, :], XB[:, :], ACT.Exp, scale=-1.0))
                nc.scalar.activation(XB[:, :], XB[:, :], ACT.Ln, bias=1.0).then_inc(soft_ready, 1)
                split2(n + 8)
                evacuated(act, t + (-1))
                sigmoid_for_dve(n + 7, t + 3)
                act.wait_ge(s_ready, i + 1)
                nc.scalar.activation(XB[:, :], XA[:, :], ACT.Exp).then_inc(a_ready, 1)

            head(0, True)
            with act.Fori(1, SB_IT) as i:
                head(i, False)
            steps.end(SB_IT)
            gated_hi(16)

            act.wait_ge(glo_ready, 16)
            act.wait_ge(av_done, SB_IT)
            steps.begin(0, 2)
            steps.link(nc.scalar.activation(softp, if_rows[:, :], ACT.Abs))
            steps.link(nc.scalar.activation(softp, softp, ACT.Exp, scale=-1.0))
            steps.end(1)
            nc.scalar.activation(softp, softp, ACT.Ln, bias=1.0).then_inc(gate_act, 1)
            act.wait_ge(gate_dve, 4 + 2 * MLH)
            nc.scalar.activation(EM[:, :, :], EM[:, :, :], ACT.Exp).then_inc(gate_act, 1)
            nc.scalar.activation(wend[:, :, :], wend[:, :, :], ACT.Exp).then_inc(gate_act, 1)
            nc.scalar.activation(decay[:, :], decay[:, :], ACT.Exp).then_inc(gate_act, 1)
            nc.scalar.activation(wi[:, :, :], wi[:, :, :], ACT.Exp).then_inc(gate_act, 1)

            with act.Fori(0, ML_IT) as i:
                n, t = At(H_ML, i, ML_HALVES), At(T_ML, i, ML_TILES)
                split2(n + 2)
                split2(n + 4)
                act.wait_ge(D_ready, i + 1)
                nc.scalar.activation(XA[:, 0:ML_W], XA[:, 0:ML_W], ACT.Exp).then_inc(W_ready, 1)
                for c in range(3, 8):
                    split2(n + 2 * c)
                act.wait_ge(w_used, (n + 13).value(1))
                nc.scalar.activation(two(og[:, 0, :]), pair(t + 6), ACT.Sigmoid).then_inc(psum_free[(t + 6).base % 2], 1)
                split2(n + 16)
                act.wait_ge(w_used, (n + 15).value(1))
                nc.scalar.activation(two(og[:, 1, :]), pair(t + 7), ACT.Sigmoid).then_inc(psum_free[(t + 7).base % 2], 1)
                act.wait_ge(num_ready, i + 1)
                nc.scalar.activation(den[:, :], den[:, :], ACT.Abs).then_inc(dabs_ready, 1)
                nc.scalar.activation(XA[:, 0:MC * T].rearrange("p (c t) -> p c t", c=MC), num[:, :, :], ACT.Square
                                     ).then_inc(squares_ready, 1)
                split2(n + 18)
                evacuated(act, t + (-1))
                sigmoid_for_dve(n + 17, t + 8)
                act.wait_ge(dmax_ready, i + 1)
                nc.scalar.activation(den[:, :], den[:, :], ACT.Square, scale=EPS ** 0.5).then_inc(dsq_ready, 1)
                split2(n + 20)
                evacuated(act, t + 8)
                sigmoid_for_dve(n + 19, t + 9)
                act.wait_ge(ssq_read, i + 1)
                nc.scalar.activation(den[:, :], den[:, :], ACT.Sqrt).then_inc(root_ready, 1)
                gated_hi(i * 2 + 17)
                gated_hi(i * 2 + 18)

            act.wait_ge(state_ready, MLH + 1)
            with act.Fori(0, NBR) as b:
                with act.Fori(0, 4) as dd:
                    it = b * 4 + dd
                    n, t = At(H_MG, it, MG_HALVES), At(T_MG, it, MG_TILES)
                    for j in range(4):
                        split_hi(n + (3 * j + 2))
                        evacuated(act, t + (2 * j - 1))
                        act.wait_ge(w_used, (n + (3 * j + 1)).value(1))
                        nc.scalar.activation(two(gsig[:, :]), pair(t + 2 * j), ACT.Sigmoid
                                             ).then_inc(psum_free[(t + 2 * j).base % 2], 1)
                        split2(n + (3 * j + 3))
            act.wait_ge(branch_done, NBR * KD)
            for k in range(KD):
                nc.scalar.activation(x_hi[:, k, :], merged[:, k, :], ACT.Copy).then_inc(mhi_ready, 1)

            def out_tiles(d, is_first, is_last):
                n, t = At(H_OUT, d, OUT_HALVES), At(T_OUT, d, OUT_TILES)
                nr = At(0, d, OUT_TILES)
                for j in range(2):
                    if not (is_last and j == 1):
                        split2(n + (2 * j + 2))
                    act.wait_ge(yg_ready, (nr + j).value(1))
                    if not (is_first and j == 0):
                        act.wait_ge(ysq_done, (nr + j).value())
                    for m in range(NB):
                        rows = P if m < NT else TS
                        i = nc.scalar.activation(ysq[0:rows, m, :], M[0:rows, 1024 * j + P * m:1024 * j + P * (m + 1)],
                                                 ACT.Square, accum_out=ysums[0:rows, m, bass.ds(d * 2 + j, 1)])
                    i.then_inc(ysq_done, 1)

            out_tiles(0, True, False)
            with act.Fori(1, OUT_IT - 1) as d:
                out_tiles(d, False, False)
            out_tiles(OUT_IT - 1, False, True)
            act.wait_ge(yms_ready, 1)
            nc.scalar.activation(rs_y, ss_y, ACT.Sqrt).then_inc(root_y_ready, 1)

        @block.vector
        def _(dve):
            steps = Steps(dve, dve_steps)

            def split_lo(n):
                dve.wait_ge(w_hi_ready, n.value(1))
                nc.vector.tensor_tensor(w_lo[:, n.base % RING, :, :], raw[:, n.base % RAW, :, :],
                                        w_hi[:, n.base % RING, :, :].bitcast(F32), ALU.subtract).then_inc(w_lo_ready, 1)

            def split2(n):
                split_lo(n)
                split_lo(n + 1)

            def read_tile(out, n_last, t, scale=None):
                dve.wait_ge(w_used, n_last.value(1))
                if scale is None:
                    i = nc.vector.tensor_copy(two(out), pair(t))
                else:
                    i = nc.vector.tensor_scalar(two(out), pair(t), scale, None, ALU.mult)
                i.then_inc(psum_free[t.base % 2], 1)

            def silu_tile(out, t, k):
                dve.wait_ge(sig_ready, k)
                nc.vector.tensor_tensor(two(out), pair(t), two(sig[:, :]), ALU.mult).then_inc(psum_free[t.base % 2], 1)

            def gated_lo(k):
                dve.wait_ge(ghi_ready, k)
                nc.vector.tensor_tensor(g_lo[:, :], gated[:, :], g_hi[:, :].bitcast(F32), ALU.subtract
                                        ).then_inc(glo_ready, 1)

            nc.vector.memset(small[:, 0:20], 1.0).then_inc(small_cleared, 1)
            dve.sem_inc(urow_copied, 1)
            dve.sem_inc(state_ready, 1)
            dve.wait_ge(sq_done, NB)
            nc.vector.tensor_scalar(ss_x, ss_x, 1.0 / D, EPS, ALU.mult, ALU.add).then_inc(ms_ready, 1)
            dve.wait_ge(root_x_ready, 1)
            steps.begin(0, 1)
            steps.link(nc.vector.reciprocal(rs_x, rs_x))
            steps.end(1)
            dve.wait_ge(vectors_loaded, 16 * VECTORS)
            for m in range(NB):
                rows = P if m < NT else TS
                nc.vector.scalar_tensor_tensor(xt[0:rows, m, :], xt[0:rows, m, :], rs_x[0:rows, m:m + 1],
                                               gpre_b[0:rows, :], ALU.mult, ALU.mult).then_inc(xs_ready, 1)
            split2(At(0))
            for m in range(NB):
                rows = P if m < NT else TS
                for q in range(4):
                    dve.wait_ge(xhi_done, 4 * m + q + 1)
                    nc.vector.tensor_tensor(x_lo[:, 4 * q:4 * q + 4, m * P:m * P + rows],
                                            M[:, 512 * q:512 * (q + 1)].rearrange("p (j r) -> p j r", j=4)[:, :, 0:rows],
                                            x_hi[:, 4 * q:4 * q + 4, m * P:m * P + rows].bitcast(F32),
                                            ALU.subtract).then_inc(xlo_done, 1)
            split2(At(2))
            dve.wait_ge(w_used, 2)
            nc.vector.tensor_scalar(two(if_rows[:, :]), pair(At(0))[0:ROWS], bif, None, ALU.add
                                    ).then_inc(psum_free[0], 1)
            steps.begin(0, 3)
            steps.link(nc.vector.memset(U[:, :, 0:PST + 1], 0.0))
            for j in range(PST + 1):
                last = nc.vector.memset(inv_cnt[:, j:j + 1], 1.0 / (j + 1))
            steps.link(last)
            steps.link(nc.vector.memset(state_row[:, :, 0:1], 0.0))
            steps.end(1)
            dve.wait_ge(sptr_done, 1)
            nc.vector.tensor_copy(state_row[:, :, 1:PST + 1],
                                  M[:, 0:16 * KW].rearrange("p (k s) -> p k s", k=KW)[:, :, 0:PST]).then_inc(sptr_copied, 1)
            dve.wait_ge(sptr_copied, 1)
            for g in range(POOL_IT):
                n, t = At(H_POOL + g * POOL_HALVES), At(T_POOL + g * POOL_TILES)
                w = WINDOWS[g]
                for c in range(2):
                    split2(n + (2 * c + 2))
                    dve.wait_ge(w_used, (n + (2 * c + 1)).value(1))
                    src, u = pair(t + c), U[:, c, :]
                    a, b = PST + 1, PST + 1 + TP + PST + 1
                    nc.vector.tensor_copy(u[:, a:a + TH], src[:, 0, :])
                    nc.vector.tensor_copy(u[:, a + TH:a + TP], src[:, 1, 0:TP - TH])
                    nc.vector.tensor_copy(u[:, a + TP:b], state_row[:, 2 * g + c, :])
                    nc.vector.tensor_copy(u[:, b:b + TS], src[:, 1, TP - TH:TH]).then_inc(psum_free[(t + c).base % 2], 1)
                    evacuated(dve, t + c)
                    steps.begin(0, w.bit_length())
                    at, src, lo = 0, u, 0
                    for s in range(w.bit_length() - 1):
                        lo += 1 << s
                        dst = sums[:, at, :]
                        steps.link(nc.vector.tensor_tensor(dst[:, lo:UW], src[:, lo:UW], src[:, lo - (1 << s):UW - (1 << s)], ALU.add))
                        src, at = dst, 1 - at
                    steps.link(nc.vector.tensor_tensor(first[:, 0:w], src[:, a:a + w], inv_cnt[:, 0:w], ALU.mult))
                    steps.end(1)
                    nc.vector.tensor_tensor(pooled[:, c, 0:w], first[:, 0:w], u[:, a:a + w], ALU.subtract)
                    nc.vector.scalar_tensor_tensor(pooled[:, c, w:TP], src[:, a + w:a + TP], 1.0 / w, u[:, a + w:a + TP],
                                                   ALU.mult, ALU.subtract)
                    nc.vector.scalar_tensor_tensor(pooled[:, c, TP:T], src[:, b:b + TS], 1.0 / w, u[:, b:b + TS],
                                                   ALU.mult, ALU.subtract).then_inc(pooled_ready, 1)
                split2(n + 6)
                silu_tile(silu[:, 0, :], t + 2, 2 * g + 1)
                evacuated(dve, t + 2)
                dve.wait_ge(wpool_done, g + 2)
                if g:
                    dve.wait_ge(glo_ready, 2 * g)
                for c in range(2):
                    if c == 1:
                        split2(n + 8)
                        silu_tile(silu[:, 1, :], t + 3, 2 * g + 2)
                        evacuated(dve, t + 3)
                    mixed = M[:, 1024 * c:1024 * (c + 1)].rearrange("p (b t) -> p b t", b=2)[:, :, 0:TH]
                    nc.vector.scalar_tensor_tensor(two(gated[:, :]), mixed, pscale[:, 2 * g + c:2 * g + c + 1],
                                                   two(silu[:, c, :]), ALU.mult, ALU.mult).then_inc(g_ready, 1)
                    gated_lo(2 * g + c + 1)
                dve.wait_ge(urow_done, g + 1)
                if g:
                    dve.wait_ge(urow_stored, 32 * g)
                nc.vector.tensor_copy(pool_row[:, :], M[0:PST, 0:4 * P]).then_inc(urow_copied, 1)

            def gate_head(k):
                dve.wait_ge(av_done, k - 8)
                nc.vector.tensor_tensor(gated[:, 0:TP], M[:, 1536:2048], silu[:, 0, 0:TP], ALU.mult)
                nc.vector.tensor_tensor(gated[:, TP:T], M[:, 1024:1024 + TS], silu[:, 0, TP:T], ALU.mult
                                        ).then_inc(g_ready, 1)
                gated_lo(k)

            def head(i, is_first):
                n, t = At(H_SB, i, SB_HALVES), At(T_SB, i, SB_TILES)
                steps.begin(i, 1)
                split2(n + 2)
                read_tile(kT[:, 0, :], n + 1, t)
                if not is_first:
                    gate_head(i + 8)
                split2(n + 4)
                read_tile(qT[:, 0, :], n + 3, t + 1, DH ** -0.5)
                dve.wait_ge(ktr_done, i + 1)
                if not is_first:
                    dve.wait_ge(k_stored, i * 32)
                nc.vector.tensor_copy(k_tok[:, :], M[:, 0:(NB + 1) * P]).then_inc(ktok_ready, 1)
                split2(n + 6)
                read_tile(vT[:, 0, :], n + 5, t + 2)
                dve.wait_ge(z_done, i + 1)
                nc.vector.tensor_copy(XA[:, :], M[:, 0:SB_W]).then_inc(zs_ready, 1)
                dve.wait_ge(soft_ready, i + 1)
                nc.vector.scalar_tensor_tensor(XC[:, :], XA[:, :], 0.0, XB[:, :], ALU.max, ALU.add).then_inc(L_ready, 1)
                split2(n + 8)
                silu_tile(silu[:, 0, :], t + 3, i + 9)
                dve.wait_ge(after_done, i + 1)
                if not is_first:
                    dve.wait_ge(v_stored, i * 32)
                nc.vector.tensor_copy(v_tok[:, :], M[:, SB_W:SB_W + NB * P]).then_inc(vtok_ready, 1)
                steps.link(nc.vector.tensor_tensor(XA[:, :], M[:, 0:SB_W], XA[:, :], ALU.add))
                nc.vector.tensor_scalar(XA[:, :], XA[:, :], 0.0, None, ALU.min).then_inc(s_ready, 1)

            dve.wait_ge(urow_stored, 32 * POOL_IT)
            head(0, True)
            with dve.Fori(1, SB_IT) as i:
                head(i, False)
            steps.end(SB_IT)
            gate_head(16)

            dve.wait_ge(gate_act, 1)
            nc.vector.scalar_tensor_tensor(lf, if_rows[:, :], 0.0, softp, ALU.min, ALU.subtract).then_inc(gate_dve, 1)
            steps.begin(0, 5)
            steps.link(nc.vector.memset(onesrow, 1.0))
            dve.wait_ge(gate_pe, 1)
            steps.link(nc.vector.tensor_copy(two(fsel), M[0:MLH, 0:1024].rearrange("p (b t) -> p b t", b=2)[:, :, 0:TH]))
            for a, b in ((0, TP), (TP, T)):
                last = nc.vector.tensor_tensor_scan(fcum[:, a:b], onesrow[:, a:b], fsel[:, a:b], 0.0, ALU.mult, ALU.add)
            steps.link(last)
            steps.link(nc.vector.tensor_tensor(arow, if_rows[0:MLH, :], fcum, ALU.subtract))
            for a, b, m0 in ((0, TP, 0.0), (TP, T, m0row)):
                last = nc.vector.tensor_tensor_scan(grow[:, a:b], arow[:, a:b], arow[:, a:b], m0, ALU.max, ALU.max)
            steps.link(last)
            steps.end(1)
            nc.vector.tensor_tensor(frow, fcum, grow, ALU.add).then_inc(gate_dve, 1)
            dve.wait_ge(gate_pe, 2)
            dve.wait_ge(k_stored, 32 * SB_IT)
            dve.wait_ge(v_stored, 32 * SB_IT)
            nc.vector.tensor_copy(acol[:, :, :].rearrange("p j h -> p (j h)"), M[:, 1024:1024 + NB * MLH]).then_inc(gate_dve, 1)
            for h in range(MLH):
                for r in range(2):
                    dve.wait_ge(gate_pe, 3 + 2 * h + r)
                    src = M[:, 1024 * r:1024 * (r + 1)].rearrange("p (b t) -> p b t", b=2)[:, :, 0:TH]
                    if r == 0:
                        i = nc.vector.tensor_copy(two(NG[:, h, :]), src)
                    else:
                        i = nc.vector.tensor_scalar(two(EM[:, h, :]), src, EM_MAX, None, ALU.min)
                    i.then_inc(gate_dve, 1)
            dve.wait_ge(gate_dve, 3 + 2 * MLH)
            dve.wait_ge(gate_loads, 32)
            for h in range(MLH):
                for lo, hi, tl in ((0, NT, TP - 1), (NT, NB, T - 1)):
                    nc.vector.tensor_scalar(wend[:, h, lo:hi], acol[:, lo:hi, h], NG[:, h, tl:tl + 1], 0.0, ALU.add, ALU.min)
                nc.vector.tensor_scalar(decay[:, h:h + 1], m0b[:, h:h + 1], NG[:, h, T - 1:T], None, ALU.add)
                i = nc.vector.tensor_scalar(wi[:, h, :], NG[:, h, TP:T], m0b[:, h:h + 1], None, ALU.add)
            i.then_inc(gate_dve, 1)
            dve.wait_ge(gate_act, 5)
            steps.begin(0, 2)
            steps.link(nc.vector.memset(wend[0:TS, :, NT:NB], 0.0))
            steps.link(nc.vector.memset(mv_tok[:, :, MDH:MDH + 1], 1.0))
            steps.end(1)

            with dve.Fori(0, ML_IT) as i:
                n, t = At(H_ML, i, ML_HALVES), At(T_ML, i, ML_TILES)
                steps.begin(i, 7)
                split2(n + 2)
                read_tile(qT[:, 0, :], n + 1, t)
                split2(n + 4)
                dve.wait_ge(m_out, 1)
                for kb, col, w, q0 in ML_BLOCKS:
                    last = nc.vector.tensor_scalar(XA[:, col:col + w], NG[:, bass.ds(i, 1), q0:q0 + w],
                                                   acol[:, kb, bass.ds(i, 1)], 0.0, ALU.add, ALU.min)
                last.then_inc(D_ready, 1)
                read_tile(qT[:, 1, :], n + 3, t + 1)
                split2(n + 6)
                read_tile(kT[:, 0, :], n + 5, t + 2)
                split2(n + 8)
                read_tile(kT[:, 1, :], n + 7, t + 3)
                split2(n + 10)
                read_tile(vT[:, 0, :], n + 9, t + 4)
                dve.wait_ge(mktr_done, i + 1)
                nc.vector.tensor_copy(mk_tok[:, :, :].rearrange("p j d -> p (j d)"), M[:, 0:NB * MDH]).then_inc(mktok_ready, 1)
                dve.wait_ge(mktok_ready, i + 1)
                for kb in range(NB):
                    last = nc.vector.tensor_scalar(mk_tok[:, kb, :], mk_tok[:, kb, :], wend[:, bass.ds(i, 1), kb],
                                                   MDH ** -0.5, ALU.mult, ALU.mult)
                last.then_inc(kw_ready, 1)
                for c in range(MC):
                    nc.vector.tensor_tensor(qw[:, c, :], qT[:, c, TP:T], wi[:, bass.ds(i, 1), :], ALU.mult)
                    nc.vector.tensor_scalar(n0b[:, c, :], ones[:, :], n0[:, bass.ds(i * MC + c, 1)], None, ALU.mult)
                split2(n + 12)
                read_tile(vT[:, 1, :], n + 11, t + 5)
                dve.wait_ge(scores_done, i + 1)
                dve.wait_ge(Wm_ready, i + 1)
                dve.wait_ge(states_out, i + 1)
                nc.vector.tensor_tensor(XB[:, 0:ML_W], M[:, 0:ML_W], XA[:, 0:ML_W], ALU.mult).then_inc(sw_ready, 1)
                split2(n + 14)
                dve.wait_ge(mvtr_done, i + 1)
                nc.vector.tensor_copy(mv_tok[:, :, 0:MDH], M[:, 0:NB * MDH].rearrange("p (j d) -> p j d", j=NB)
                                      ).then_inc(mvtok_ready, 1)
                split2(n + 16)
                dve.wait_ge(num_done, i + 1)
                nc.vector.tensor_copy(num[:, :, 0:TP], M[:, 0:2 * TP].rearrange("p (c t) -> p c t", c=MC))
                nc.vector.tensor_copy(num[:, :, TP:T], M[:, 1536:1536 + MC * TS].rearrange("p (c t) -> p c t", c=MC))
                nc.vector.tensor_copy(den[:, 0:TP], M[:, 1024:1536])
                nc.vector.tensor_copy(den[:, TP:T], M[:, 1536 + MC * TS:1536 + (MC + 1) * TS]).then_inc(num_ready, 1)
                split2(n + 18)
                dve.wait_ge(dabs_ready, i + 1)
                nc.vector.scalar_tensor_tensor(den[:, :], den[:, :], DEN_MIN, EM[:, bass.ds(i, 1), :].rearrange("p a t -> p (a t)"),
                                               ALU.max, ALU.max).then_inc(dmax_ready, 1)
                silu_tile(silu[:, 0, :], t + 8, i * 2 + 17)
                evacuated(dve, t + 8)
                steps.link(nc.vector.tensor_tensor(silu[:, 0, :], silu[:, 0, :], og[:, 0, :], ALU.mult))
                dve.wait_ge(ssq_done, i + 1)
                dve.wait_ge(dsq_ready, i + 1)
                nc.vector.scalar_tensor_tensor(two(den[:, :]), M[:, 0:1024].rearrange("p (b t) -> p b t", b=2)[:, :, 0:TH],
                                               1.0 / MDH, two(den[:, :]), ALU.mult, ALU.add).then_inc(ssq_read, 1)
                split2(n + 20)
                dve.wait_ge(root_ready, i + 1)
                steps.link(nc.vector.reciprocal(den[:, :], den[:, :]))
                silu_tile(silu[:, 1, :], t + 9, i * 2 + 18)
                evacuated(dve, t + 9)
                steps.link(nc.vector.tensor_tensor(silu[:, 1, :], silu[:, 1, :], og[:, 1, :], ALU.mult))
                for c in range(MC):
                    steps.link(nc.vector.tensor_tensor(num[:, c, :], num[:, c, :], den[:, :], ALU.mult))
                    nc.vector.scalar_tensor_tensor(gated[:, :], num[:, c, :], hnorm[:, bass.ds(i * MC + c, 1)],
                                                   silu[:, c, :], ALU.mult, ALU.mult).then_inc(g_ready, 1)
                    gated_lo(i * 2 + (17 + c))
                dve.wait_ge(state_done, i + 1)
                new = M[:, :].rearrange("p (s c v) -> p s c v", s=2, c=MC)
                nc.vector.tensor_copy(XB[:, 0:MC * MDH].rearrange("p (c v) -> p c v", c=MC), new[:, 0, :, 0:MDH])
                nc.vector.tensor_copy(n_out[:, 0, bass.ds(i * MC, MC)], new[:, 0, :, MDH:MDH + 1].rearrange("p c v -> p (c v)"))
                steps.link(nc.vector.tensor_scalar(n0b[:, 0, 0:MC], n0[:, bass.ds(i * MC, MC)], decay[:, bass.ds(i, 1)], None, ALU.mult))
                steps.link(nc.vector.tensor_tensor(n_out[:, 1, bass.ds(i * MC, MC)], new[:, 1, :, MDH:MDH + 1].rearrange("p c v -> p (c v)"),
                                                   n0b[:, 0, 0:MC], ALU.add))
                nc.vector.scalar_tensor_tensor(XB[:, MC * MDH:2 * MC * MDH].rearrange("p (c v) -> p c v", c=MC), c0[:, :, :],
                                               decay[:, bass.ds(i, 1)], new[:, 1, :, 0:MDH], ALU.mult, ALU.add
                                               ).then_inc(state_ready, 1)
            steps.end(ML_IT)

            dve.wait_ge(merged_zero, 1)
            with dve.Fori(0, NBR) as b:
                with dve.Fori(0, 4) as dd:
                    it = b * 4 + dd
                    n, t = At(H_MG, it, MG_HALVES), At(T_MG, it, MG_TILES)
                    for j in range(4):
                        split_lo(n + (3 * j + 2))
                        split2(n + (3 * j + 3))
                        evacuated(dve, t + 2 * j)
                        dve.wait_ge(w_used, (n + (3 * j + 2)).value(1))
                        nc.vector.tensor_tensor(two(term[:, :]), pair(t + (2 * j + 1)), two(gsig[:, :]), ALU.mult
                                                ).then_inc(psum_free[(t + (2 * j + 1)).base % 2], 1)
                        evacuated(dve, t + (2 * j + 1))
                        m = merged[:, bass.ds(dd * 4 + j, 1), :].rearrange("p a t -> p (a t)")
                        nc.vector.tensor_tensor(m, m, term[:, :], ALU.add).then_inc(branch_done, 1)
            for k in range(KD):
                dve.wait_ge(mhi_ready, k + 1)
                nc.vector.tensor_tensor(x_lo[:, k, :], merged[:, k, :], x_hi[:, k, :].bitcast(F32), ALU.subtract
                                        ).then_inc(mlo_ready, 1)
            steps.begin(0, 1)
            steps.link(nc.vector.memset(ysums[:, :, :], 1.0))
            steps.end(1)
            dve.wait_ge(late_loads, 16 * 3)

            def out_tiles(d, is_first, is_last):
                n, t = At(H_OUT, d, OUT_HALVES), At(T_OUT, d, OUT_TILES)
                nr = At(0, d, OUT_TILES)
                for j in range(2):
                    if not (is_last and j == 1):
                        split2(n + (2 * j + 2))
                    if not (is_first and j == 0):
                        dve.wait_ge(ytr_done, (nr + j).value())
                    read_tile(yT[:, :], n + (2 * j + 1), t + j)
                    dve.wait_ge(ytr_done, (nr + j).value(1))
                    for m in range(NB):
                        rows = P if m < NT else TS
                        col = d * (2 * P) + j * P
                        last = nc.vector.tensor_tensor(y_tok[0:rows, m, bass.ds(col, P)],
                                                       M[0:rows, 1024 * j + P * m:1024 * j + P * (m + 1)],
                                                       gpost_b[0:rows, bass.ds(col, P)], ALU.mult)
                    last.then_inc(yg_ready, 1)

            out_tiles(0, True, False)
            with dve.Fori(1, OUT_IT - 1) as d:
                out_tiles(d, False, False)
            out_tiles(OUT_IT - 1, False, True)
            dve.wait_ge(ysq_done, KD)
            steps.begin(0, 2)
            steps.link(nc.vector.tensor_reduce(ss_y, ysums[:, :, :], AXX, ALU.add))
            nc.vector.tensor_scalar(ss_y, ss_y, 1.0 / D, EPS, ALU.mult, ALU.add).then_inc(yms_ready, 1)
            dve.wait_ge(root_y_ready, 1)
            steps.link(nc.vector.reciprocal(rs_y, rs_y))
            steps.end(1)
            for m in range(NB):
                rows = P if m < NT else TS
                nc.vector.scalar_tensor_tensor(y_tok[0:rows, m, :], y_tok[0:rows, m, :], rs_y[0:rows, m:m + 1],
                                               x_again[0:rows, m, :], ALU.mult, ALU.add).then_inc(yout_ready, 1)

        @block.gpsimd
        def _(pool):
            steps = Steps(pool, pool_steps)

            def own_wait():
                pool.sem_inc(pool_turns, 1)

            pool.sem_inc(states_out, 1)
            for m in range(NB):
                if m < NT:
                    pool.dma_start(xt[:, m, :], xp_v[:, m, :]).then_inc(x_loaded[m], 16)
                else:
                    pool.dma_start(xt[0:TS, m, :], x_sample[0, :, :]).then_inc(x_loaded[m], 16)
            vectors = [(gpre_b[:, :], g_pre[0, :].partition_broadcast(P)),
                       (hnorm[:, :], ml_hnorm.rearrange("a (k p) -> p (a k)", p=P)),
                       (pscale[:, :], pool_scale.rearrange("a (k p) -> p (a k)", p=P)),
                       (bif, b_if.rearrange("a r h -> (r h) a")),
                       (m0row, state_ml_m.rearrange("a b h -> h (a b)"))]
            assert len(vectors) == VECTORS
            for dst, src in vectors:
                pool.dma_start(dst, src, allow_slow_non_contiguous=True).then_inc(vectors_loaded, 16)
            steps.begin(0, 2)
            steps.link(nc.gpsimd.memset(ident[:, :], 0.0))
            nc.gpsimd.affine_select(ident[:, :], ident[:, :], pattern=[[-1, P]], compare_op=ALU.not_equal, fill=1.0,
                                    base=0, channel_multiplier=1).then_inc(consts_ready, 1)
            nc.gpsimd.memset(ones[:, :], 1.0).then_inc(consts_ready, 1)
            nc.gpsimd.memset(negones[:, :], -1.0).then_inc(consts_ready, 1)
            steps.link(nc.gpsimd.memset(negtri[:, :], -1.0))
            nc.gpsimd.affine_select(negtri[:, :], negtri[:, :], pattern=[[-1, P]], compare_op=ALU.is_ge, fill=0.0,
                                    base=0, channel_multiplier=1).then_inc(consts_ready, 1)
            steps.end(1)

            def build_mask(blocks, width, value, strict):
                own = [x for x in blocks if x[0] != "past"]
                steps.begin(0, 1 + len(own) + 1)
                steps.link(nc.gpsimd.memset(mask[:, 0:width], value))
                for kb, col, w, q0 in own:
                    w = min(w, P)
                    steps.link(nc.gpsimd.affine_select(mask[:, col:col + w], mask[:, col:col + w], pattern=[[1, w]],
                                                       compare_op=ALU.is_gt if strict else ALU.is_ge, fill=0.0,
                                                       base=q0 - TOKEN0[kb], channel_multiplier=-1))
                kb, col, w, q0 = own[-1]
                steps.link(nc.gpsimd.affine_select(mask[:, col:col + w], mask[:, col:col + w], pattern=[[0, w]],
                                                   compare_op=ALU.is_ge, fill=0.0, base=-TS, channel_multiplier=1))
                steps.end(1)

            def store_gated(k, tile_nr):
                pool.wait_ge(glo_ready, k)
                for s, src in enumerate((g_hi, g_lo)):
                    pool.dma_start(gated_v[:, s, bass.ds(tile_nr, 1), :].rearrange("p a t -> p (a t)"), src[:, :]
                                   ).then_inc(g_stored, 16)

            pool.wait_ge(xlo_done, 4 * NB)
            pool.dma_start(spool[:, :], state_pool[0, 0, :, :]).then_inc(spool_loaded, 16)
            with pool.Fori(0, POOL_IT) as g:
                pool.wait_ge(wpool_done, g + 1)
                pool.dma_start(wp[:, :, :, :], w_pool_v[:, bass.ds(g, 1), :, :]).then_inc(wp_loaded, 16)
                store_gated(g * 2 + 1, g * 2)
                store_gated(g * 2 + 2, g * 2 + 1)
                pool.wait_ge(urow_copied, g + 2)
                rows = pool_row[:, :].rearrange("t (c s d) -> t c s d", c=2, s=2)
                for s, dst in enumerate((p_pool_v, s_pool_v)):
                    pool.dma_start(dst[:, bass.ds(g * (2 * P), 2 * P)].rearrange("t (c d) -> t c d", c=2), rows[:, :, s, :]
                                   ).then_inc(urow_stored, 16)
            pool.wait_ge(urow_stored, 32 * POOL_IT)
            build_mask(SB_BLOCKS, SB_W, 1.0, True)

            def head(i, is_first):
                if not is_first:
                    pool.wait_ge(ktr_done, i * 1)
                pool.dma_start(past_k[:, :], past_k_v[:, bass.ds(i * P, P)]).then_inc(past_k_loaded, 16)
                if not is_first:
                    store_gated(i + 8, i + 7)
                pool.dma_start(past_v[:, :], past_v_v[:, bass.ds(i * P, P)]).then_inc(past_v_loaded, 16)
                pool.wait_ge(ktok_ready, i + 1)
                own_wait()
                pool.dma_start(pk_v[:, :, bass.ds(i * P, P)], k_tok[:, 0:NT * P].rearrange("p (m d) -> p m d", m=NT)
                               ).then_inc(k_stored, 16)
                pool.dma_start(sk_v[:, bass.ds(i * P, P)], k_tok[TS:P, NT * P:NB * P]).then_inc(k_stored, 16)
                pool.wait_ge(L_ready, i + 1)
                nc.gpsimd.tensor_tensor(XC[:, :], XC[:, :], mask[:, :], ALU.mult).then_inc(Lm_ready, 1)
                pool.wait_ge(a_ready, i + 1)
                nc.gpsimd.tensor_tensor(XB[:, :], XB[:, :], mask[:, :], ALU.mult).then_inc(am_ready, 1)
                pool.dma_start(pv_v[:, :, bass.ds(i * P, P)], v_tok[:, P:NB * P].rearrange("p (m d) -> p m d", m=NT)
                               ).then_inc(v_stored, 16)
                pool.dma_start(sv_v[:, bass.ds(i * P, P)], v_tok[TS:P, 0:P]).then_inc(v_stored, 16)

            head(0, True)
            with pool.Fori(1, SB_IT) as i:
                head(i, False)
            store_gated(16, 15)

            pool.wait_ge(av_done, SB_IT)
            steps.begin(0, 2)
            steps.link(nc.gpsimd.memset(XB[0:MLH, 0:MLH * P], 0.0))
            nc.gpsimd.affine_select(negsel, negsel, pattern=[[-1, MLH], [0, P]], compare_op=ALU.not_equal, fill=-1.0,
                                    base=0, channel_multiplier=1).then_inc(sel_ready, 1)
            steps.link(nc.gpsimd.memset(selF, 0.0))
            nc.gpsimd.affine_select(selF, selF, pattern=[[-1, MLH]], compare_op=ALU.not_equal, fill=1.0,
                                    base=-MLH, channel_multiplier=1).then_inc(sel_ready, 1)
            steps.end(1)
            pool.wait_ge(k_stored, 32 * SB_IT)
            pool.wait_ge(v_stored, 32 * SB_IT)
            pool.dma_start(m0b[:, :], state_ml_m[0, 0, :].partition_broadcast(P)).then_inc(gate_loads, 16)
            pool.dma_start(n0[:, :], n0_v, allow_slow_non_contiguous=True).then_inc(gate_loads, 16)
            build_mask(ML_BLOCKS, ML_W, MDH ** -0.5, False)
            pool.wait_ge(gate_dve, 2)
            pool.dma_start(p_m.rearrange("a b h -> h (a b)"), frow[:, TP - 1:TP], allow_slow_non_contiguous=True).then_inc(m_stored, 16)
            pool.dma_start(s_m.rearrange("a b h -> h (a b)"), frow[:, T - 1:T], allow_slow_non_contiguous=True).then_inc(m_stored, 16)
            pool.wait_ge(m_stored, 32)
            pool.sem_inc(m_out, 1)

            with pool.Fori(0, ML_IT) as i:
                pool.wait_ge(state_ready, i + 1)
                pool.dma_start(c0[:, :, :], c0_v[:, i, :, :]).then_inc(c0_loaded, 16)
                pool.wait_ge(W_ready, i + 1)
                nc.gpsimd.tensor_tensor(XA[:, 0:ML_W], XA[:, 0:ML_W], mask[:, 0:ML_W], ALU.mult).then_inc(Wm_ready, 1)
                store_gated(i * 2 + 17, i * 2 + 16)
                store_gated(i * 2 + 18, i * 2 + 17)
                pool.wait_ge(state_ready, i + 2)
                own_wait()
                for s, dst in enumerate((p_c_v, s_c_v)):
                    pool.dma_start(dst[:, i, :, :], XB[:, s * MC * MDH:(s + 1) * MC * MDH].rearrange("p (c v) -> p c v", c=MC)
                                   ).then_inc(state_stored, 16)
                pool.wait_ge(state_stored, i * 32 + 32)
                pool.sem_inc(states_out, 1)
            pool.dma_start(p_n_v, n_out[:, 0, :], allow_slow_non_contiguous=True).then_inc(n_stored, 16)
            pool.dma_start(s_n_v, n_out[:, 1, :], allow_slow_non_contiguous=True).then_inc(n_stored, 16)
            pool.wait_ge(n_stored, 32)
            pool.wait_ge(state_stored, 32 * ML_IT)
            pool.wait_ge(g_stored, 32 * NBR * KW)

            nc.gpsimd.memset(merged[:, :, :], 0.0).then_inc(merged_zero, 1)
            pool.dma_start(gpost_b[:, :], g_post[0, :].partition_broadcast(P)).then_inc(late_loads, 16)
            with pool.Fori(0, NBR) as b:
                pool.wait_ge(w_used, b * (4 * MG_HALVES) + H_MG)
                for s, dst in enumerate((gt_hi, gt_lo)):
                    pool.dma_start(dst[:, :, :], gated_v[:, s, bass.ds(b * KW, KW), :]).then_inc(gt_loaded, 16)
            pool.wait_ge(mlo_ready, KD)
            pool.dma_start(x_again[:, 0:NT, :], xp_v).then_inc(late_loads, 16)
            pool.dma_start(x_again[0:TS, NT, :], x_sample[0, :, :]).then_inc(late_loads, 16)


_INS = ["x_prompt", "x_sample", "cache_sb_k", "cache_sb_v", "state_pool", "state_ml_c", "state_ml_n", "state_ml_m",
        "g_pre", "w_in", "b_if", "w_pool", "pool_scale", "ml_hnorm", "w_branch", "w_out", "g_post"]
_OUTS = [(1, TP, D), (1, TS, D), (1, 1, TP, SBH, DH), (1, 1, TP, SBH, DH), (1, 1, PST, W), (1, 1, MLH, MDH, MDH),
         (1, 1, MLH, MDH), (1, 1, MLH), (1, 1, TS, SBH, DH), (1, 1, TS, SBH, DH), (1, 1, PST, W),
         (1, 1, MLH, MDH, MDH), (1, 1, MLH, MDH), (1, 1, MLH)]


def kernel(**inputs):
    import numpy as _np
    import concourse.bacc as _bacc
    from concourse import mybir as _mybir
    from concourse.bass_utils import run_bass_kernel_spmd as _run

    nc = _bacc.Bacc("TRN2", target_bir_lowering=False, num_devices=1)
    arrays, args = {}, []
    for name in _INS:
        a = _np.ascontiguousarray(inputs[name])
        arrays[f"in_{name}_dram"] = a
        args.append(nc.dram_tensor(f"in_{name}_dram", a.shape, _mybir.dt.from_np(a.dtype), kind="ExternalInput").ap())
    for i, shape in enumerate(_OUTS):
        args.append(nc.dram_tensor(f"out_{i}_dram", shape, _mybir.dt.float32, kind="ExternalOutput").ap())
    hybrid_layer(nc, *args)
    r = _run(nc, [arrays], core_ids=[0])
    return tuple(r.results[0][f"out_{i}_dram"] for i in range(len(_OUTS)))
```

```python
import concourse.bass as bass
from concourse import mybir
from contextlib import ExitStack

F32 = mybir.dt.float32
F32R = mybir.dt.float32r
ALU = mybir.AluOpType
ACT = mybir.ActivationFunctionType
AXX = mybir.AxisListType.X

P = 128
D = 2048
KD = D // P
W = 1024
KW = W // P
TP, TS = 512, 64
T = TP + TS
TH = T // 2
PAST = 128
SBH, DH = 8, 128
MLH, MDH = 4, 256
MC = MDH // P
PG = 4
WINDOWS = (2, 4, 8, 16)
PST = 15
EPS = 1e-6
NBR = 3
OFF_POOL, OFF_SQ, OFF_SK, OFF_SV = 0, W, 2 * W, 3 * W
OFF_MQ, OFF_MK, OFF_MV, OFF_MO, OFF_MI = 4 * W, 5 * W, 6 * W, 7 * W, 8 * W
OFF_Z = OFF_MI + 2 * MLH
OFF_G = OFF_Z + NBR * W
NT = TP // P
NB = NT + 1
UW = 2 * (PST + 1) + T

HK = 8
RAW, RING = 2, 4

POOL_IT, POOL_HALVES, POOL_TILES = PG, 8, 4
SB_IT, SB_HALVES, SB_TILES = SBH, 8, 4
ML_IT, ML_HALVES, ML_TILES = MLH, 20, 10
MG_IT, MG_HALVES, MG_TILES = NBR * 4, 12, 8
OUT_IT, OUT_HALVES, OUT_TILES = KD // 2, 4, 2
H_POOL, T_POOL = 2, 1
H_SB, T_SB = H_POOL + POOL_IT * POOL_HALVES, T_POOL + POOL_IT * POOL_TILES
H_ML, T_ML = H_SB + SB_IT * SB_HALVES, T_SB + SB_IT * SB_TILES
H_MG, T_MG = H_ML + ML_IT * ML_HALVES, T_ML + ML_IT * ML_TILES
H_OUT, T_OUT = H_MG + MG_IT * MG_HALVES, T_MG + MG_IT * MG_TILES

SB_BLOCKS = [(0, 0, 512, 0), (1, 512, 384, 128), (3, 896, 128, 384), (2, 1024, 256, 256),
             ("past", 1280, 64, TP), (4, 1344, 64, TP)]
SB_W = 1408
ML_BLOCKS = [(0, 0, 512, 0), (1, 512, 384, 128), (3, 896, 128, 384), (2, 1024, 256, 256),
             (4, 1280, 64, TP)]
ML_W = 1344
SB_MASKED = [(0, 0, 128), (512, 128, 128), (896, 256, 256), (1344, 512, 64)]
ML_MASKED = [(0, 0, 128), (512, 128, 128), (896, 256, 256), (1280, 512, 64)]
MASK_KEYS = [0, 1, 3, 2, 4]
MASK_W = 576
TOKEN0 = [0, 128, 256, 384, T - P]


EM_MAX = 45.0
DEN_MIN = 1e-14
VECTORS = 4
GATE_LOADS = 4


POOLS_BLOCKS = [2, 3, 4]


class At:

    def __init__(self, base, i=0, per=0):
        self.base, self.i, self.per = base, i, per

    def __add__(self, n):
        return At(self.base + n, self.i, self.per)

    def value(self, plus=0):
        return self.i * self.per + (self.base + plus)

    def count(self, slots):
        assert self.per % slots == 0
        return self.i * (self.per // slots) + (self.base // slots + 1)


class Steps:

    def __init__(self, eng, sem):
        self.eng, self.sem, self.base, self.i, self.per, self.k = eng, sem, 0, 0, 0, 0

    def begin(self, i, per):
        self.i, self.per, self.k = i, per, 0

    def end(self, times):
        assert self.k == self.per, (self.k, self.per)
        self.base += self.per * times

    def link(self, ins):
        self.k += 1
        ins.then_inc(self.sem, 1)
        self.eng.wait_ge(self.sem, self.i * self.per + (self.base + self.k))


def hybrid_layer(nc, x_prompt, x_sample, cache_sb_k, cache_sb_v, state_pool, state_ml_c, state_ml_n,
                 state_ml_m, g_pre, w_in, b_if, w_pool, pool_scale, ml_hnorm, w_branch, w_out, g_post,
                 y_prompt, y_sample, p_k, p_v, p_pool, p_c, p_n, p_m, s_k, s_v, s_pool, s_c, s_n, s_m):
    w_in_v = w_in.rearrange("a (k p) c -> p (a k) c", p=P)
    w_br_v = w_branch.rearrange("a b (k p) c -> p (a b) k c", p=P)
    w_out_v = w_out.rearrange("a (k p) c -> p (a k) c", p=P)
    w_pool_v = w_pool.rearrange("a g (k p) c -> p (a g) k c", p=P)
    c0_v = state_ml_c.rearrange("a b h (k p) v -> p (a b h) k v", p=P)
    n0_v = state_ml_n.rearrange("a b h (k p) -> p (a b h k)", p=P)
    p_c_v = p_c.rearrange("a b h (k p) v -> p (a b h) k v", p=P)
    s_c_v = s_c.rearrange("a b h (k p) v -> p (a b h) k v", p=P)
    p_n_v = p_n.rearrange("a b h (k p) -> p (a b h k)", p=P)
    s_n_v = s_n.rearrange("a b h (k p) -> p (a b h k)", p=P)
    xp_v = x_prompt.rearrange("a (m p) d -> p (a m) d", p=P)
    yp_v = y_prompt.rearrange("a (m p) d -> p (a m) d", p=P)
    pk_v = p_k.rearrange("a b (m p) h d -> p (a b m) (h d)", p=P)
    pv_v = p_v.rearrange("a b (m p) h d -> p (a b m) (h d)", p=P)
    sk_v = s_k.rearrange("a b t h d -> (a b t) (h d)")
    sv_v = s_v.rearrange("a b t h d -> (a b t) (h d)")
    past_k_v = cache_sb_k.rearrange("a b t h d -> (a b t) (h d)")
    past_v_v = cache_sb_v.rearrange("a b t h d -> (a b t) (h d)")
    p_pool_v = p_pool.rearrange("a b t c -> (a b t) c")
    s_pool_v = s_pool.rearrange("a b t c -> (a b t) c")
    gated_dram = nc.dram_tensor("gated_scratch", (2 * NBR * KW * P, T), F32R, kind="Internal").ap()
    rows_dram = nc.dram_tensor("rows_scratch", (2, MLH * T), F32, kind="Internal").ap()
    gated_v = gated_dram.rearrange("(s k p) t -> p s k t", s=2, p=P)

    ctx = ExitStack()
    with ctx:
        def sb(name, shape, dt=F32, where=ctx):
            return where.enter_context(nc.sbuf_tensor(name, shape, dt))

        def sem(name):
            return ctx.enter_context(nc.semaphore(name))

        x_hi = sb("x_hi", [P, KD, T], F32R)
        x_lo = sb("x_lo", [P, KD, T], F32R)
        raw = sb("raw", [P, RAW, HK, P])
        w_hi = sb("w_hi", [P, RING, HK, P], F32R)
        w_lo = sb("w_lo", [P, RING, HK, P], F32R)
        ident = sb("ident", [P, P])
        ones = sb("ones", [P, P])
        negones = sb("negones", [P, P], F32R)
        negtri = sb("negtri", [P, P], F32R)
        small = sb("small", [P, 24])
        hnorm = sb("hnorm", [P, KW])
        pscale = sb("pscale", [P, KW])

        with ExitStack() as e:
            xt = sb("xt", [P, NB, D], where=e)
            gpre_b = sb("gpre_b", [P, D], where=e)
            junk = sb("junk", [P, D], where=e)
            negones_f = sb("negones_f", [P, P], where=e)
            negtri_f = sb("negtri_f", [P, P], where=e)
        with ExitStack() as e:
            g_hi = sb("g_hi", [P, T], F32R, where=e)
            g_lo = sb("g_lo", [P, T], F32R, where=e)
            sig = sb("sig", [P, T], where=e)
            gated = sb("gated", [P, T], where=e)
            silu = sb("silu", [P, 2, T], where=e)
            wi = sb("wi", [P, MLH, TS], where=e)
            acol = sb("acol", [P, NB, MLH], where=e)
            wend = sb("wend", [P, MLH, NB], where=e)
            m0b = sb("m0b", [P, MLH], where=e)
            decay = sb("decay", [P, MLH], where=e)
            n0 = sb("n0", [P, MLH * MC], where=e)
            G = sb("G", [P, MLH, T], where=e)
            EM = sb("EM", [P, MLH, T], where=e)
            with ExitStack() as e2:
                U = sb("U", [P, 2, UW], where=e2)
                sums = sb("sums", [P, 2, UW], where=e2)
                pooled = sb("pooled", [P, 2, T], where=e2)
                first = sb("first", [P, PST + 1], where=e2)
                inv_cnt = sb("inv_cnt", [P, PST + 1], where=e2)
                wp = sb("wp", [P, 1, 2, 2 * P], where=e2)
                spool = sb("spool", [PST, W], where=e2)
                pool_row = sb("pool_row", [PST, 4 * P], where=e2)
                state_row = sb("state_row", [P, KW, PST + 1], where=e2)
                if_rows = sb("if_rows", [2 * MLH, T], where=e2)
                softp = sb("softp", [2 * MLH, T], where=e2)
                lf = sb("lf", [2 * MLH, T], where=e2)
                fsel = sb("fsel", [MLH, T], where=e2)
                fcum = sb("fcum", [MLH, T], where=e2)
                arow = sb("arow", [MLH, T], where=e2)
                grow = sb("grow", [MLH, T], where=e2)
                frow = sb("frow", [MLH, T], where=e2)
            mask = sb("mask", [P, MASK_W], where=e)
            XA = sb("XA", [P, SB_W], where=e)
            qT = sb("qT", [P, MC, T], where=e)
            vT = sb("vT", [P, MC, T], where=e)
            kT = sb("kT", [P, MC, T], where=e)
            with ExitStack() as e2:
                XB = sb("XB", [P, SB_W], where=e2)
                XC = sb("XC", [P, SB_W], where=e2)
                XC_hi = sb("XC_hi", [P, SB_W], F32R, where=e2)
                XC_lo = sb("XC_lo", [P, SB_W], F32R, where=e2)
                k_tok = sb("k_tok", [P, (NB + 1) * P], where=e2)
                v_tok = sb("v_tok", [P, NB * P], where=e2)
                past_k = sb("past_k", [P, P], where=e2)
                past_v = sb("past_v", [P, P], where=e2)
            with ExitStack() as e2:
                S_hi = sb("S_hi", [P, ML_W], F32R, where=e2)
                S_lo = sb("S_lo", [P, ML_W], F32R, where=e2)
                mk_hi = sb("mk_hi", [P, NB, MDH], F32R, where=e2)
                mk_lo = sb("mk_lo", [P, NB, MDH], F32R, where=e2)
                mv_hi = sb("mv_hi", [P, NB, MDH + 2], F32R, where=e2)
                mv_lo = sb("mv_lo", [P, NB, MDH + 2], F32R, where=e2)
                ones_r = sb("ones_r", [P, P], F32R, where=e2)
                c0 = sb("c0", [P, MC, MDH], where=e2)
                num = sb("num", [P, MC, T], where=e2)
                n_decayed = sb("n_decayed", [P, MC], where=e2)
                n_out = sb("n_out", [P, 2, MLH * MC], where=e2)
        with ExitStack() as e:
            gsig = sb("gsig", [P, 2, T], where=e)
            term = sb("term", [P, 2, T], where=e)
            beside = [2 * T, MLH * TS, NB * MLH, NB * MLH, MLH, MLH, MLH * MC]
            sb("beside", [P, sum(-(-w // 8) * 8 for w in beside)], where=e)
            gt_hi = sb("gt_hi", [P, KW, T], F32R, where=e)
            gt_lo = sb("gt_lo", [P, KW, T], F32R, where=e)
            merged = sb("merged", [P, KD, T], where=e)
        with ExitStack() as e:
            x_again = sb("x_again", [P, NB, D], where=e)
            y_tok = sb("y_tok", [P, NB, D], where=e)
            yT = sb("yT", [P, T], where=e)
            ysq = sb("ysq", [P, NB, P], where=e)
            ysums = sb("ysums", [P, NB, KD], where=e)
            gpost_b = sb("gpost_b", [P, D], where=e)

        ROWS = 2 * MLH
        og, den = kT, vT[:, 0, :]
        states = num[:, :, :].rearrange("p c t -> p (c t)")
        qw = vT[:, 1, 0:MC * TS].rearrange("p (c t) -> p c t", c=MC)
        n0b = vT[:, 1, MC * TS:MC * (TS + P)].rearrange("p (c j) -> p c j", c=MC)
        ss_x, rs_x = small[:, 0:NB], small[:, NB:2 * NB]
        ss_y, rs_y = small[:, 10:10 + NB], small[:, 15:15 + NB]
        bif, m0row = small[0:ROWS, 20:21], small[0:MLH, 21:22]

        pp = ctx.enter_context(nc.psum_tensor("pp", [P, 4, 512], F32))
        M = ctx.enter_context(nc.psum_tensor("M", [P, 4 * 512], F32))

        def x_bank(m, q):
            return M[:, 512 * q:512 * (q + 1)] if m % 2 == 0 else pp[:, q, :]

        def pair(t):
            return pp[:, 2 * (t.base % 2):2 * (t.base % 2) + 2, 0:TH]

        def two(ap):
            return ap.rearrange("p (b t) -> p b t", b=2)

        def evacuated(eng, t):
            eng.wait_ge(psum_free[t.base % 2], t.count(2))

        w_loaded = [sem(f"w_loaded{r}") for r in range(RAW)]
        w_hi_ready, w_lo_ready, w_used = sem("w_hi_ready"), sem("w_lo_ready"), sem("w_used")
        psum_free = [sem("psum_free0"), sem("psum_free1")]
        dve_steps, act_steps, pool_steps = sem("dve_steps"), sem("act_steps"), sem("pool_steps")
        x_loaded = [sem(f"x_loaded{m}") for m in range(NB)]
        gain_loaded, vectors_loaded, consts_ready, signs_ready, small_cleared = sem("gain_loaded"), sem("vectors_loaded"), sem("consts_ready"), sem("signs_ready"), sem("small_cleared")
        sq_done, ms_ready, root_x_ready = sem("sq_done"), sem("ms_ready"), sem("root_x_ready")
        xg_ready = sem("xg_ready")
        xs_ready, xtr_done, xhi_done, xlo_done = sem("xs_ready"), sem("xtr_done"), sem("xhi_done"), sem("xlo_done")
        pool_turns, states_out = sem("pool_turns"), sem("states_out")
        sig_ready, dabs_ready = sem("sig_ready"), sem("dabs_ready")
        g_ready, ghi_ready, glo_ready, g_stored = sem("g_ready"), sem("ghi_ready"), sem("glo_ready"), sem("g_stored")
        spool_loaded, sptr_done, sptr_copied = sem("spool_loaded"), sem("sptr_done"), sem("sptr_copied")
        wp_loaded, pooled_ready, wpool_done = sem("wp_loaded"), sem("pooled_ready"), sem("wpool_done")
        urow_copied, urow_stored = sem("urow_copied"), sem("urow_stored")
        past_k_loaded, past_v_loaded = sem("past_k_loaded"), sem("past_v_loaded")
        ktr_done, ktok_ready, k_stored = sem("ktr_done"), sem("ktok_ready"), sem("k_stored")
        z_done, zs_ready, soft_ready = sem("z_done"), sem("zs_ready"), sem("soft_ready")
        L_ready, Lm_ready, after_done = sem("L_ready"), sem("Lm_ready"), sem("after_done")
        xchi_ready, xclo_ready = sem("xchi_ready"), sem("xclo_ready")
        vtok_ready, v_stored, s_ready = sem("vtok_ready"), sem("v_stored"), sem("s_ready")
        a_ready, am_ready, av_done = sem("a_ready"), sem("am_ready"), sem("av_done")
        gate_dve, gate_act, gate_pe, fsel_loaded = sem("gate_dve"), sem("gate_act"), sem("gate_pe"), sem("fsel_loaded")
        gate_loads, m_stored, rows_stored = sem("gate_loads"), sem("m_stored"), sem("rows_stored")
        c0_loaded, mktr_done, mkhi_ready, kw_ready = sem("c0_loaded"), sem("mktr_done"), sem("mkhi_ready"), sem("kw_ready")
        D_ready, W_ready, Wm_ready = sem("D_ready"), sem("W_ready"), sem("Wm_ready")
        scores_done, sw_ready, mvtr_done, mvtok_ready = sem("scores_done"), sem("sw_ready"), sem("mvtr_done"), sem("mvtok_ready")
        shi_ready, slo_ready, mvhi_ready = sem("shi_ready"), sem("slo_ready"), sem("mvhi_ready")
        num_done, num_ready, squares_ready = sem("num_done"), sem("num_ready"), sem("squares_ready")
        dmax_ready, dsq_ready, ssq_done, ssq_read, root_ready = sem("dmax_ready"), sem("dsq_ready"), sem("ssq_done"), sem("ssq_read"), sem("root_ready")
        state_done, state_ready, state_stored, n_stored = sem("state_done"), sem("state_ready"), sem("state_stored"), sem("n_stored")
        gt_loaded, merged_free, branch_done = sem("gt_loaded"), sem("merged_free"), sem("branch_done")
        mhi_ready, mlo_ready = sem("mhi_ready"), sem("mlo_ready")
        gain_y_loaded, x_again_loaded = sem("gain_y_loaded"), sem("x_again_loaded")
        ytr_done, yg_ready, ysq_done = sem("ytr_done"), sem("yg_ready"), sem("ysq_done")
        yms_ready, root_y_ready, yout_ready, y_stored = sem("yms_ready"), sem("root_y_ready"), sem("yout_ready"), sem("y_stored")

        block = ctx.enter_context(nc.Block())

        @block.sync
        def _(sp):
            def load(n, src):
                if n.base >= RAW:
                    sp.wait_ge(w_lo_ready, n.value(1 - RAW))
                slot = n.base % RAW
                sp.dma_start(raw[:, slot, :, :], src).then_inc(w_loaded[slot], 16)

            def load_tile(n, col):
                load(n, w_in_v[:, 0:HK, bass.ds(col, P)])
                load(n + 1, w_in_v[:, HK:2 * HK, bass.ds(col, P)])

            for m in range(NT):
                sp.dma_start(xt[:, m, :], xp_v[:, m, :]).then_inc(x_loaded[m], 16)
                if m == 0:
                    sp.dma_start(gpre_b[:, :], g_pre[0, :].partition_broadcast(P)).then_inc(gain_loaded, 16)
            sp.dma_start(xt[0:TS, NT, :], x_sample[0, :, :]).then_inc(x_loaded[NT], 16)
            load_tile(At(0), OFF_MI)
            with sp.Fori(0, POOL_IT) as g:
                n = At(H_POOL, g, POOL_HALVES)
                for c, off in enumerate([OFF_POOL, OFF_POOL + P, OFF_Z, OFF_Z + P]):
                    load_tile(n + 2 * c, g * (2 * P) + off)
            with sp.Fori(0, SB_IT) as h:
                n = At(H_SB, h, SB_HALVES)
                for c, off in enumerate([OFF_SK, OFF_SQ, OFF_SV, OFF_Z + W]):
                    load_tile(n + 2 * c, h * P + off)
            with sp.Fori(0, ML_IT) as h:
                n = At(H_ML, h, ML_HALVES)
                for c, off in enumerate([OFF_MQ, OFF_MK, OFF_MV, OFF_MO, OFF_Z + 2 * W]):
                    for j in range(MC):
                        load_tile(n + (2 * MC * c + 2 * j), h * MDH + (off + j * P))
            with sp.Fori(0, NBR) as b:
                with sp.Fori(0, 4) as dd:
                    n = At(H_MG, b * 4 + dd, MG_HALVES)
                    for j in (0, 2):
                        for c in range(2):
                            load_tile(n + (3 * j + 2 * c), b * D + dd * (4 * P) + (OFF_G + (j + c) * P))
                        for c in range(2):
                            load(n + (3 * j + 4 + c), w_br_v[:, b, :, bass.ds(dd * (4 * P) + (j + c) * P, P)])
            with sp.Fori(0, OUT_IT) as d:
                n = At(H_OUT, d, OUT_HALVES)
                for j in range(2):
                    for s in range(2):
                        load(n + (2 * j + s), w_out_v[:, s * HK:(s + 1) * HK, bass.ds(d * (2 * P) + j * P, P)])
            for m in range(NB):
                sp.wait_ge(yout_ready, m + 1)
                if m < NT:
                    sp.dma_start(yp_v[:, m, :], y_tok[:, m, :]).then_inc(y_stored, 16)
                else:
                    sp.dma_start(y_sample[0, :, :], y_tok[0:TS, m, :]).then_inc(y_stored, 16)
            sp.wait_ge(y_stored, 16 * NB)

        @block.tensor
        def _(pe):
            def half(n, t, xh, xl, k0, opens, closes):
                pe.wait_ge(w_lo_ready, n.value(1))
                if opens and t.base >= 2:
                    evacuated(pe, t + (-2))
                slot, out = n.base % RING, pair(t)
                for k in range(HK):
                    for s, (ws, xs) in enumerate(((w_hi, xh), (w_hi, xl), (w_lo, xh))):
                        for b in range(2):
                            i = nc.tensor.matmul(
                                out[:, b, :], ws[:, slot, k, :], xs[:, k0 + k, b * TH:(b + 1) * TH],
                                start=opens and k == 0 and s == 0, stop=closes and k == HK - 1 and s == 2)
                i.then_inc(w_used, 1)

            def tile(n, t):
                half(n, t, x_hi, x_lo, 0, True, False)
                half(n + 1, t, x_hi, x_lo, HK, False, True)

            def transposes(blocks):
                for out, src in blocks:
                    k = src.shape[0]
                    i = nc.tensor.transpose(out, src, ident[0:k, 0:k])
                return i

            pe.sem_inc(wpool_done, 1)
            pe.wait_ge(consts_ready, 4)
            for m in range(NB):
                rows = P if m < NT else TS
                pe.wait_ge(xs_ready, m + 1)
                for q in range(4):
                    if m >= 2:
                        pe.wait_ge(xlo_done, 4 * m + q - 7)
                    transposes([(x_bank(m, q)[:, P * j:P * j + rows],
                                 xt[0:rows, m, (4 * q + j) * P:(4 * q + j + 1) * P]) for j in range(4)]
                               ).then_inc(xtr_done, 1)
            pe.wait_ge(xlo_done, 4 * NB)
            tile(At(0), At(0))
            pe.wait_ge(spool_loaded, 16)
            transposes([(M[:, 16 * j:16 * j + PST], spool[0:PST, j * P:(j + 1) * P]) for j in range(KW)]
                       ).then_inc(sptr_done, 1)
            pe.wait_ge(sptr_copied, 1)
            with pe.Fori(0, POOL_IT) as g:
                n, t = At(H_POOL, g, POOL_HALVES), At(T_POOL, g, POOL_TILES)
                tile(n, t)
                tile(n + 2, t + 1)
                tile(n + 4, t + 2)
                pe.wait_ge(pooled_ready, g * 2 + 2)
                pe.wait_ge(wp_loaded, g * 16 + 16)
                pe.wait_ge(urow_copied, g + 1)
                transposes([(M[0:PST, 512 * (2 * c + s) + TH:512 * (2 * c + s) + TH + P], U[:, c, o:o + PST])
                            for c in range(2) for s, o in enumerate((1 + TP, UW - PST))])
                for c in range(2):
                    for b in range(2):
                        for k in range(2):
                            i = nc.tensor.matmul(M[:, 1024 * c + 512 * b:1024 * c + 512 * b + TH],
                                                 wp[:, 0, k, c * P:(c + 1) * P],
                                                 pooled[:, k, b * TH:(b + 1) * TH], start=k == 0, stop=k == 1)
                i.then_inc(wpool_done, 1)
                tile(n + 6, t + 3)

            def weigh_values(prev):
                pe.wait_ge(am_ready, prev + 1)
                pe.wait_ge(vtok_ready, prev + 1)
                pe.wait_ge(past_v_loaded, prev * 16 + 16)
                for s, (kb, col, w, q0) in enumerate(SB_BLOCKS[:4]):
                    nc.tensor.matmul(M[:, 1536 + q0:1536 + q0 + w], v_tok[:, (kb + 1) * P:(kb + 2) * P],
                                     XB[:, col:col + w], start=s == 0, stop=s == 3)
                nc.tensor.matmul(M[:, 1024:1024 + TS], past_v[:, :], XB[:, 1280:1344], start=True, stop=False)
                nc.tensor.matmul(M[:, 1024:1024 + TS], v_tok[:, 0:P], XB[:, 1344:1408], start=False, stop=True
                                 ).then_inc(av_done, 1)

            def head(i, is_first):
                n, t = At(H_SB, i, SB_HALVES), At(T_SB, i, SB_TILES)
                tile(n, t)
                if is_first:
                    pe.wait_ge(urow_copied, POOL_IT + 1)
                    pe.wait_ge(gate_dve, 2)
                    transposes([(M[:, MLH * j:MLH * (j + 1)], arow[:, TOKEN0[j]:TOKEN0[j] + P]) for j in range(NB)]
                               ).then_inc(gate_pe, 1)
                else:
                    weigh_values(i - 1)
                half(n + 2, t + 1, x_hi, x_lo, 0, True, False)
                evacuated(pe, t)
                pe.wait_ge(past_k_loaded, i * 16 + 16)
                if is_first:
                    pe.wait_ge(gate_dve, 3)
                else:
                    pe.wait_ge(s_ready, i * 1)
                transposes([(M[:, j * P:(j + 1) * P], kT[:, 0, TOKEN0[j]:TOKEN0[j] + P]) for j in range(NB)]
                           + [(M[:, NB * P:(NB + 1) * P], past_k[:, :])]).then_inc(ktr_done, 1)
                half(n + 3, t + 1, x_hi, x_lo, HK, False, True)
                half(n + 4, t + 2, x_hi, x_lo, 0, True, False)
                evacuated(pe, t + 1)
                pe.wait_ge(ktok_ready, i + 1)
                pe.wait_ge(g_ready, i + 8)
                for kb, col, w, q0 in SB_BLOCKS:
                    keys = k_tok[:, NB * P:(NB + 1) * P] if kb == "past" else kT[:, 0, TOKEN0[kb]:TOKEN0[kb] + P]
                    m = nc.tensor.matmul(M[:, col:col + w], keys, qT[:, 0, q0:q0 + w], start=True, stop=True)
                m.then_inc(z_done, 1)
                half(n + 5, t + 2, x_hi, x_lo, HK, False, True)
                tile(n + 6, t + 3)
                pe.wait_ge(xclo_ready, i + 1)
                evacuated(pe, t + 2)
                if is_first:
                    pe.wait_ge(signs_ready, 2)
                at = {kb: (col, w, q0) for kb, col, w, q0 in SB_BLOCKS}
                for kb, col, w, q0 in SB_BLOCKS:
                    later = [4] if kb == "past" else [x for x in range(NT) if kb < x] if kb < NT else []
                    terms = [(negtri, col, w, q0)] + [(negones, *at[x]) for x in later]
                    for x, (signs, c2, w2, q2) in enumerate(terms):
                        for part in (XC_hi, XC_lo):
                            nc.tensor.matmul(M[:, col + q2 - q0:col + q2 - q0 + w2], signs[:, :], part[:, c2:c2 + w2],
                                             start=x == 0 and part is XC_hi, stop=x == len(terms) - 1 and part is XC_lo)
                transposes([(M[:, SB_W:SB_W + P], vT[:, 0, TOKEN0[4]:TOKEN0[4] + P])]
                           + [(M[:, 1536 + j * P:1536 + (j + 1) * P], vT[:, 0, TOKEN0[j]:TOKEN0[j] + P])
                              for j in range(NT)]).then_inc(after_done, 1)

            head(0, True)
            with pe.Fori(1, SB_IT) as i:
                head(i, False)
            tile(At(H_ML), At(T_ML))
            weigh_values(SB_IT - 1)
            def ml_head(i, is_first):
                n, t = At(H_ML, i, ML_HALVES), At(T_ML, i, ML_TILES)
                for c in range(1 if is_first else 0, 5):
                    tile(n + 2 * c, t + c)
                evacuated(pe, t + 3)
                evacuated(pe, t + 2)
                pe.wait_ge(g_ready, 16)
                pe.wait_ge(state_ready, i + 1)
                transposes([(M[:, MDH * j + P * c:MDH * j + P * (c + 1)], kT[:, c, TOKEN0[j]:TOKEN0[j] + P])
                            for j in range(NB) for c in range(MC)]).then_inc(mktr_done, 1)
                tile(n + 10, t + 5)
                pe.wait_ge(kw_ready, i + 1)
                for kb, col, w, q0 in ML_BLOCKS:
                    for c in range(MC):
                        m = nc.tensor.matmul(M[:, col:col + w], kT[:, c, TOKEN0[kb]:TOKEN0[kb] + P],
                                             qT[:, c, q0:q0 + w], start=c == 0, stop=c == MC - 1)
                m.then_inc(scores_done, 1)
                tile(n + 12, t + 6)
                evacuated(pe, t + 4)
                evacuated(pe, t + 5)
                pe.wait_ge(sw_ready, i + 1)
                transposes([(M[:, MDH * j + P * c:MDH * j + P * (c + 1)], vT[:, c, TOKEN0[j]:TOKEN0[j] + P])
                            for j in range(NB) for c in range(MC)]).then_inc(mvtr_done, 1)
                tile(n + 14, t + 7)
                pe.wait_ge(slo_ready, i + 1)
                pe.wait_ge(mvtok_ready, i + 1)
                pe.wait_ge(c0_loaded, i * 16 + 16)

                def weigh(out, kb, v, col, w, opens, closes):
                    if v == 2:
                        terms = [(ones_r[:, :], S_hi), (ones_r[:, :], S_lo)]
                    else:
                        cols = slice(v * P, (v + 1) * P)
                        terms = [(mv_hi[:, kb, cols], S_hi), (mv_lo[:, kb, cols], S_hi), (mv_hi[:, kb, cols], S_lo)]
                    for s, (lhs, S) in enumerate(terms):
                        nc.tensor.matmul(out, lhs, S[:, col:col + w], start=opens and s == 0,
                                         stop=closes and s == len(terms) - 1)

                for v in range(3):
                    for s, (kb, col, w, q0) in enumerate(ML_BLOCKS[:4]):
                        weigh(M[:, 512 * v + q0:512 * v + q0 + w], kb, v, col, w, s == 0, s == 3)
                for v in range(3):
                    out = M[:, 1536 + TS * v:1536 + TS * (v + 1)]
                    weigh(out, 4, v, 1280, TS, True, False)
                    for c in range(MC):
                        lhs = n0b[:, c, :] if v == 2 else c0[:, c, v * P:(v + 1) * P]
                        m = nc.tensor.matmul(out, lhs, qw[:, c, :], start=False, stop=c == MC - 1)
                m.then_inc(num_done, 1)
                tile(n + 16, t + 8)
                pe.wait_ge(squares_ready, i + 1)
                for b in range(2):
                    for c in range(MC):
                        m = nc.tensor.matmul(M[:, 512 * b:512 * b + TH], ones[:, :],
                                             XA[:, c * T + b * TH:c * T + (b + 1) * TH], start=c == 0, stop=c == MC - 1)
                m.then_inc(ssq_done, 1)
                tile(n + 18, t + 9)
                pe.wait_ge(ssq_read, i + 1)
                for c in range(MC):
                    for stream, blocks in enumerate((range(NT), [NT])):
                        out = M[:, 1024 * stream + 512 * c:1024 * stream + 512 * c + MDH + 2]
                        for kb in blocks:
                            for s, (mk, mv) in enumerate(((mk_hi, mv_hi), (mk_hi, mv_lo), (mk_lo, mv_hi))):
                                m = nc.tensor.matmul(out, mk[:, kb, c * P:(c + 1) * P], mv[:, kb, :],
                                                     start=kb == blocks[0] and s == 0, stop=kb == blocks[-1] and s == 2)
                m.then_inc(state_done, 1)

            ml_head(0, True)
            with pe.Fori(1, ML_IT) as i:
                ml_head(i, False)

            with pe.Fori(0, NBR) as b:
                with pe.Fori(0, 4) as dd:
                    it = b * 4 + dd
                    n, t = At(H_MG, it, MG_HALVES), At(T_MG, it, MG_TILES)
                    for j in (0, 2):
                        for c in range(2):
                            tile(n + (3 * j + 2 * c), t + (2 * j + c))
                        if j == 0:
                            pe.wait_ge(gt_loaded, b * 32 + 32)
                        for c in range(2):
                            half(n + (3 * j + 4 + c), t + (2 * j + 2 + c), gt_hi, gt_lo, 0, True, True)

            def to_tokens(t, nr, is_first):
                evacuated(pe, t)
                if not is_first:
                    pe.wait_ge(ysq_done, nr.value())
                at = 1024 * (nr.base % 2)
                transposes([(M[:, at + P * m:at + P * (m + 1)], yT[:, m * P:(m + 1) * P]) for m in range(NT)]
                           + [(M[0:TS, at + 512:at + 640], yT[:, TP:T])]).then_inc(ytr_done, 1)

            def out_tiles(d, is_first):
                n, t, nr = At(H_OUT + 4, d - 1, OUT_HALVES), At(T_OUT + 2, d - 1, OUT_TILES), At(2, d - 1, OUT_TILES)
                if is_first:
                    n, t, nr = At(H_OUT), At(T_OUT), At(0)
                for j in range(2):
                    for s in range(2):
                        if is_first and j == 0:
                            pe.wait_ge(mlo_ready, HK * (s + 1))
                        half(n + (2 * j + s), t + j, x_hi, x_lo, s * HK, s == 0, s == 1)
                        if s == 0 and not (is_first and j == 0):
                            to_tokens(t + (j - 1), nr + (j - 1), is_first)

            pe.wait_ge(state_ready, MLH + 1)
            out_tiles(0, True)
            with pe.Fori(1, OUT_IT) as d:
                out_tiles(d, False)
            to_tokens(At(T_OUT + KD - 1), At(KD - 1), False)

        @block.scalar
        def _(act):
            steps = Steps(act, act_steps)

            def split_hi(n):
                act.wait_ge(w_loaded[n.base % RAW], n.count(RAW) * 16)
                if n.base >= RING:
                    act.wait_ge(w_used, n.value(1 - RING))
                nc.scalar.activation(w_hi[:, n.base % RING, :, :], raw[:, n.base % RAW, :, :], ACT.Copy
                                     ).then_inc(w_hi_ready, 1)

            def split2(n):
                split_hi(n)
                split_hi(n + 1)

            def sigmoid_for_dve(n_last, t):
                act.wait_ge(w_used, n_last.value(1))
                nc.scalar.activation(two(sig[:, :]), pair(t), ACT.Sigmoid).then_inc(sig_ready, 1)

            def gated_hi(k):
                act.wait_ge(g_ready, k)
                if not (isinstance(k, int) and k == 1):
                    act.wait_ge(g_stored, (k - 1) * 32)
                nc.scalar.activation(g_hi[:, :], gated[:, :], ACT.Copy).then_inc(ghi_ready, 1)

            def square(m):
                rows = P if m < NT else TS
                act.wait_ge(x_loaded[m], 16)
                if m:
                    act.wait_ge(sq_done, m)
                nc.scalar.activation(junk[0:rows, :], xt[0:rows, m, :], ACT.Square,
                                     accum_out=ss_x[0:rows, m:m + 1]).then_inc(sq_done, 1)

            def root(m):
                act.wait_ge(ms_ready, m + 1)
                nc.scalar.activation(rs_x[:, m:m + 1], ss_x[:, m:m + 1], ACT.Sqrt).then_inc(root_x_ready, 1)

            def x_parts(m):
                rows = P if m < NT else TS
                for q in range(4):
                    act.wait_ge(xtr_done, 4 * m + q + 1)
                    nc.scalar.activation(x_hi[:, 4 * q:4 * q + 4, m * P:m * P + rows],
                                         x_bank(m, q).rearrange("p (j r) -> p j r", j=4)[:, :, 0:rows],
                                         ACT.Copy).then_inc(xhi_done, 1)

            act.wait_ge(small_cleared, 1)
            square(0)
            root(0)
            square(1)
            root(1)
            square(2)
            root(2)
            x_parts(0)
            square(3)
            root(3)
            x_parts(1)
            square(4)
            root(4)
            x_parts(2)
            split2(At(0))
            x_parts(3)
            x_parts(4)
            split2(At(2))
            act.wait_ge(psum_free[0], 1)
            steps.begin(0, 2)
            steps.link(nc.scalar.activation(softp[:, :], if_rows[:, :], ACT.Abs))
            steps.link(nc.scalar.activation(softp[:, :], softp[:, :], ACT.Exp, scale=-1.0))
            steps.end(1)
            nc.scalar.activation(softp[:, :], softp[:, :], ACT.Ln, bias=1.0).then_inc(gate_act, 1)
            def group(g):
                n, t = At(H_POOL, g, POOL_HALVES), At(T_POOL, g, POOL_TILES)
                split2(n + 2)
                split2(n + 4)
                split2(n + 6)
                evacuated(act, t + (-1))
                sigmoid_for_dve(n + 5, t + 2)
                gated_hi(g * 2 + 1)
                split2(n + 8)
                evacuated(act, t + 2)
                sigmoid_for_dve(n + 7, t + 3)
                gated_hi(g * 2 + 2)

            group(0)
            with act.Fori(1, POOL_IT) as g:
                group(g)

            def head(i, is_first):
                n, t = At(H_SB, i, SB_HALVES), At(T_SB, i, SB_TILES)
                steps.begin(i, 2)
                split2(n + 2)
                if not is_first:
                    gated_hi(i + 8)
                split2(n + 4)
                if is_first:
                    act.wait_ge(gate_dve, 4)
                    nc.scalar.activation(EM[:, :, :], EM[:, :, :], ACT.Exp, scale=-1.0).then_inc(gate_act, 1)
                    nc.scalar.activation(wend[:, :, :], wend[:, :, :], ACT.Exp).then_inc(gate_act, 1)
                    nc.scalar.activation(decay[:, :], decay[:, :], ACT.Exp).then_inc(gate_act, 1)
                    nc.scalar.activation(wi[:, :, :], wi[:, :, :], ACT.Exp, scale=-1.0).then_inc(gate_act, 1)
                split2(n + 6)
                act.wait_ge(zs_ready, i + 1)
                steps.link(nc.scalar.activation(XB[:, :], XA[:, :], ACT.Abs))
                steps.link(nc.scalar.activation(XB[:, :], XB[:, :], ACT.Exp, scale=-1.0))
                nc.scalar.activation(XB[:, :], XB[:, :], ACT.Ln, bias=1.0).then_inc(soft_ready, 1)
                split2(n + 8)
                act.wait_ge(Lm_ready, i + 1)
                nc.scalar.activation(XC_hi[:, :], XC[:, :], ACT.Copy).then_inc(xchi_ready, 1)
                evacuated(act, t + (-1))
                sigmoid_for_dve(n + 7, t + 3)
                act.wait_ge(s_ready, i + 1)
                nc.scalar.activation(XB[:, :], XA[:, :], ACT.Exp).then_inc(a_ready, 1)

            head(0, True)
            with act.Fori(1, SB_IT) as i:
                head(i, False)
            steps.end(SB_IT)
            split2(At(H_ML + 2))
            gated_hi(16)

            with act.Fori(0, ML_IT) as i:
                n, t = At(H_ML, i, ML_HALVES), At(T_ML, i, ML_TILES)
                split2(n + 4)
                act.wait_ge(D_ready, i + 1)
                nc.scalar.activation(XA[:, 0:ML_W], XA[:, 0:ML_W], ACT.Exp, scale=-1.0).then_inc(W_ready, 1)
                for c in range(3, 6):
                    split2(n + 2 * c)
                act.wait_ge(mktr_done, i + 1)
                for kb in range(NB):
                    k = nc.scalar.activation(mk_hi[:, kb, :], M[:, MDH * kb:MDH * (kb + 1)], ACT.Copy,
                                             scale=wend[:, bass.ds(i, 1), kb])
                k.then_inc(mkhi_ready, 1)
                split2(n + 12)
                split2(n + 14)
                act.wait_ge(sw_ready, i + 1)
                nc.scalar.activation(S_hi[:, :], XA[:, 0:ML_W], ACT.Copy).then_inc(shi_ready, 1)
                act.wait_ge(w_used, (n + 13).value(1))
                nc.scalar.activation(two(og[:, 0, :]), pair(t + 6), ACT.Sigmoid).then_inc(psum_free[(t + 6).base % 2], 1)
                act.wait_ge(mvtr_done, i + 1)
                nc.scalar.activation(mv_hi[:, :, 0:MDH], M[:, 0:NB * MDH].rearrange("p (j d) -> p j d", j=NB), ACT.Copy
                                     ).then_inc(mvhi_ready, 1)
                split2(n + 16)
                act.wait_ge(w_used, (n + 15).value(1))
                nc.scalar.activation(two(og[:, 1, :]), pair(t + 7), ACT.Sigmoid).then_inc(psum_free[(t + 7).base % 2], 1)
                act.wait_ge(num_ready, i + 1)
                nc.scalar.activation(den, den, ACT.Abs).then_inc(dabs_ready, 1)
                nc.scalar.activation(XA[:, 0:MC * T].rearrange("p (c t) -> p c t", c=MC), num[:, :, :], ACT.Square
                                     ).then_inc(squares_ready, 1)
                split2(n + 18)
                evacuated(act, t + (-1))
                sigmoid_for_dve(n + 17, t + 8)
                act.wait_ge(dmax_ready, i + 1)
                nc.scalar.activation(den, den, ACT.Square, scale=EPS ** 0.5).then_inc(dsq_ready, 1)
                split2(n + 20)
                evacuated(act, t + 8)
                sigmoid_for_dve(n + 19, t + 9)
                act.wait_ge(ssq_read, i + 1)
                nc.scalar.activation(den, den, ACT.Sqrt).then_inc(root_ready, 1)
                gated_hi(i * 2 + 17)
                split2(n + 22)
                gated_hi(i * 2 + 18)

            def merge_tiles(it, is_first, is_last):
                n, t = At(H_MG, it, MG_HALVES), At(T_MG, it, MG_TILES)
                for j in (0, 2):
                    for c in range(2):
                        if not (is_first and c == 0 and j == 0):
                            split2(n + (3 * j + 2 + 2 * c))
                        evacuated(act, t + (2 * j + c - 2))
                        act.wait_ge(w_used, (n + (3 * j + 2 * c + 1)).value(1))
                        nc.scalar.activation(two(gsig[:, c, :]), pair(t + (2 * j + c)), ACT.Sigmoid
                                             ).then_inc(psum_free[(t + c).base % 2], 1)
                    split2(n + (3 * j + 6))
                    if is_last and j == 2:
                        act.wait_ge(branch_done, (NBR - 1) * KD - 2)
                        merged_hi(0, KD - 2)

            def merged_hi(k0, k1):
                for k in range(k0, k1):
                    nc.scalar.activation(x_hi[:, k, :], merged[:, k, :], ACT.Copy).then_inc(mhi_ready, 1)

            act.wait_ge(state_ready, MLH + 1)
            act.wait_ge(g_stored, 32 * NBR * KW)
            merge_tiles(0, True, False)
            with act.Fori(1, MG_IT - 1) as it:
                merge_tiles(it, False, False)
            merge_tiles(MG_IT - 1, False, True)
            act.wait_ge(branch_done, (NBR - 1) * KD)
            merged_hi(KD - 2, KD)

            def squares(nr, is_first):
                act.wait_ge(yg_ready, nr.value(1))
                if not is_first:
                    act.wait_ge(ysq_done, nr.value())
                for m in range(NB):
                    rows = P if m < NT else TS
                    at = 1024 * (nr.base % 2) + P * m
                    i = nc.scalar.activation(ysq[0:rows, m, :], M[0:rows, at:at + P], ACT.Square,
                                             accum_out=ysums[0:rows, m, bass.ds(nr.value(), 1)])
                i.then_inc(ysq_done, 1)

            split2(At(H_OUT + 2))
            split2(At(H_OUT + 4))
            squares(At(0), True)
            with act.Fori(0, OUT_IT - 2) as d:
                n, nr = At(H_OUT + 6, d, OUT_HALVES), At(1, d, OUT_TILES)
                for j in range(2):
                    split2(n + 2 * j)
                    squares(nr + j, False)
            split2(At(H_OUT + 2 * KD - 2))
            for nr in range(KD - 3, KD):
                squares(At(nr), False)
            act.wait_ge(yms_ready, 1)
            nc.scalar.activation(rs_y, ss_y, ACT.Sqrt).then_inc(root_y_ready, 1)

        @block.vector
        def _(dve):
            steps = Steps(dve, dve_steps)

            def split_lo(n):
                dve.wait_ge(w_hi_ready, n.value(1))
                nc.vector.tensor_tensor(w_lo[:, n.base % RING, :, :], raw[:, n.base % RAW, :, :],
                                        w_hi[:, n.base % RING, :, :].bitcast(F32), ALU.subtract).then_inc(w_lo_ready, 1)

            def split2(n):
                split_lo(n)
                split_lo(n + 1)

            def read_tile(out, n_last, t, scale=None):
                dve.wait_ge(w_used, n_last.value(1))
                if scale is None:
                    i = nc.vector.tensor_copy(two(out), pair(t))
                else:
                    i = nc.vector.tensor_scalar(two(out), pair(t), scale, None, ALU.mult)
                i.then_inc(psum_free[t.base % 2], 1)

            def silu_tile(out, t, k):
                dve.wait_ge(sig_ready, k)
                nc.vector.tensor_tensor(two(out), pair(t), two(sig[:, :]), ALU.mult).then_inc(psum_free[t.base % 2], 1)

            def gated_lo(k):
                dve.wait_ge(ghi_ready, k)
                nc.vector.tensor_tensor(g_lo[:, :], gated[:, :], g_hi[:, :].bitcast(F32), ALU.subtract
                                        ).then_inc(glo_ready, 1)

            nc.vector.memset(small[:, 0:20], 1.0).then_inc(small_cleared, 1)
            dve.sem_inc(urow_copied, 1)
            dve.sem_inc(state_ready, 1)
            dve.wait_ge(consts_ready, 4)
            nc.vector.tensor_copy(negones[:, :], negones_f[:, :]).then_inc(signs_ready, 1)
            nc.vector.tensor_copy(negtri[:, :], negtri_f[:, :]).then_inc(signs_ready, 1)
            def mean_square(m):
                dve.wait_ge(sq_done, m + 1)
                nc.vector.tensor_scalar(ss_x[:, m:m + 1], ss_x[:, m:m + 1], 1.0 / D, EPS, ALU.mult, ALU.add
                                        ).then_inc(ms_ready, 1)

            def normalise(m):
                rows = P if m < NT else TS
                dve.wait_ge(root_x_ready, m + 1)
                steps.link(nc.vector.reciprocal(rs_x[:, m:m + 1], rs_x[:, m:m + 1]))
                if m == 0:
                    dve.wait_ge(gain_loaded, 16)
                if m in POOLS_BLOCKS:
                    dve.wait_ge(xg_ready, POOLS_BLOCKS.index(m) + 1)
                    i = nc.vector.tensor_scalar(xt[0:rows, m, :], xt[0:rows, m, :], rs_x[0:rows, m:m + 1], None, ALU.mult)
                else:
                    i = nc.vector.scalar_tensor_tensor(xt[0:rows, m, :], xt[0:rows, m, :], rs_x[0:rows, m:m + 1],
                                                       gpre_b[0:rows, :], ALU.mult, ALU.mult)
                i.then_inc(xs_ready, 1)

            def x_parts(m):
                rows = P if m < NT else TS
                for q in range(4):
                    dve.wait_ge(xhi_done, 4 * m + q + 1)
                    nc.vector.tensor_tensor(x_lo[:, 4 * q:4 * q + 4, m * P:m * P + rows],
                                            x_bank(m, q).rearrange("p (j r) -> p j r", j=4)[:, :, 0:rows],
                                            x_hi[:, 4 * q:4 * q + 4, m * P:m * P + rows].bitcast(F32),
                                            ALU.subtract).then_inc(xlo_done, 1)

            steps.begin(0, NB)
            mean_square(0)
            normalise(0)
            mean_square(1)
            normalise(1)
            mean_square(2)
            x_parts(0)
            mean_square(3)
            normalise(2)
            x_parts(1)
            mean_square(4)
            normalise(3)
            x_parts(2)
            normalise(4)
            steps.end(1)
            split2(At(0))
            x_parts(3)
            x_parts(4)
            split2(At(2))
            dve.wait_ge(w_used, 2)
            dve.wait_ge(vectors_loaded, 16 * VECTORS)
            nc.vector.tensor_scalar(two(if_rows[:, :]), pair(At(0))[0:ROWS], bif, None, ALU.add
                                    ).then_inc(psum_free[0], 1)
            steps.begin(0, 3)
            steps.link(nc.vector.memset(U[:, :, 0:PST + 1], 0.0))
            for j in range(PST + 1):
                last = nc.vector.memset(inv_cnt[:, j:j + 1], 1.0 / (j + 1))
            steps.link(last)
            steps.link(nc.vector.memset(state_row[:, :, 0:1], 0.0))
            steps.end(1)
            dve.wait_ge(sptr_done, 1)
            nc.vector.tensor_copy(state_row[:, :, 1:PST + 1],
                                  M[:, 0:16 * KW].rearrange("p (k s) -> p k s", k=KW)[:, :, 0:PST]).then_inc(sptr_copied, 1)
            dve.wait_ge(sptr_copied, 1)
            def gate_rows(step):
                if step == 0:
                    dve.wait_ge(gate_act, 1)
                    nc.vector.scalar_tensor_tensor(lf[:, :], if_rows[:, :], 0.0, softp[:, :], ALU.min, ALU.subtract
                                                   ).then_inc(gate_dve, 1)
                    return
                steps.begin(0, 4)
                steps.link(nc.vector.memset(arow[:, :], 1.0))
                dve.wait_ge(fsel_loaded, 16)
                for a, b in ((0, TP), (TP, T)):
                    last = nc.vector.tensor_tensor_scan(fcum[:, a:b], arow[:, a:b], fsel[:, a:b], 0.0, ALU.mult, ALU.add)
                steps.link(last)
                steps.link(nc.vector.tensor_tensor(arow[:, :], if_rows[0:MLH, :], fcum[:, :], ALU.subtract))
                for a, b, m0 in ((0, TP, 0.0), (TP, T, m0row)):
                    last = nc.vector.tensor_tensor_scan(grow[:, a:b], arow[:, a:b], arow[:, a:b], m0, ALU.max, ALU.max)
                steps.link(last)
                steps.end(1)
                nc.vector.tensor_tensor(frow[:, :], fcum[:, :], grow[:, :], ALU.add).then_inc(gate_dve, 1)

            for g in range(POOL_IT):
                n, t = At(H_POOL + g * POOL_HALVES), At(T_POOL + g * POOL_TILES)
                w = WINDOWS[g]
                for c in range(2):
                    split2(n + (2 * c + 2))
                    dve.wait_ge(w_used, (n + (2 * c + 1)).value(1))
                    src, u = pair(t + c), U[:, c, :]
                    a, b = PST + 1, PST + 1 + TP + PST + 1
                    nc.vector.tensor_copy(u[:, a:a + TH], src[:, 0, :])
                    nc.vector.tensor_copy(u[:, a + TH:a + TP], src[:, 1, 0:TP - TH])
                    nc.vector.tensor_copy(u[:, a + TP:b], state_row[:, 2 * g + c, :])
                    nc.vector.tensor_copy(u[:, b:b + TS], src[:, 1, TP - TH:TH]).then_inc(psum_free[(t + c).base % 2], 1)
                    evacuated(dve, t + c)
                    steps.begin(0, w.bit_length())
                    at, src, lo = 0, u, 0
                    for s in range(w.bit_length() - 1):
                        lo += 1 << s
                        dst = sums[:, at, :]
                        steps.link(nc.vector.tensor_tensor(dst[:, lo:UW], src[:, lo:UW], src[:, lo - (1 << s):UW - (1 << s)], ALU.add))
                        src, at = dst, 1 - at
                    steps.link(nc.vector.tensor_tensor(first[:, 0:w], src[:, a:a + w], inv_cnt[:, 0:w], ALU.mult))
                    steps.end(1)
                    nc.vector.tensor_tensor(pooled[:, c, 0:w], first[:, 0:w], u[:, a:a + w], ALU.subtract)
                    nc.vector.scalar_tensor_tensor(pooled[:, c, w:TP], src[:, a + w:a + TP], 1.0 / w, u[:, a + w:a + TP],
                                                   ALU.mult, ALU.subtract)
                    nc.vector.scalar_tensor_tensor(pooled[:, c, TP:T], src[:, b:b + TS], 1.0 / w, u[:, b:b + TS],
                                                   ALU.mult, ALU.subtract).then_inc(pooled_ready, 1)
                    if g == 0:
                        gate_rows(c)
                split2(n + 6)
                silu_tile(silu[:, 0, :], t + 2, 2 * g + 1)
                evacuated(dve, t + 2)
                dve.wait_ge(wpool_done, g + 2)
                if g:
                    dve.wait_ge(glo_ready, 2 * g)
                for c in range(2):
                    if c == 1:
                        split2(n + 8)
                        silu_tile(silu[:, 1, :], t + 3, 2 * g + 2)
                        evacuated(dve, t + 3)
                    mixed = M[:, 1024 * c:1024 * (c + 1)].rearrange("p (b t) -> p b t", b=2)[:, :, 0:TH]
                    nc.vector.scalar_tensor_tensor(two(gated[:, :]), mixed, pscale[:, 2 * g + c:2 * g + c + 1],
                                                   two(silu[:, c, :]), ALU.mult, ALU.mult).then_inc(g_ready, 1)
                    gated_lo(2 * g + c + 1)
                if g:
                    dve.wait_ge(urow_stored, 32 * g)
                nc.vector.tensor_copy(pool_row[:, :].rearrange("t (b d) -> t b d", b=4),
                                      M[0:PST, :].rearrange("t (b c) -> t b c", b=4)[:, :, TH:TH + P]
                                      ).then_inc(urow_copied, 1)

            def gate_head(k):
                dve.wait_ge(av_done, k - 8)
                nc.vector.tensor_tensor(gated[:, 0:TP], M[:, 1536:2048], silu[:, 0, 0:TP], ALU.mult)
                nc.vector.tensor_tensor(gated[:, TP:T], M[:, 1024:1024 + TS], silu[:, 0, TP:T], ALU.mult
                                        ).then_inc(g_ready, 1)
                gated_lo(k)

            def head(i, is_first):
                n, t = At(H_SB, i, SB_HALVES), At(T_SB, i, SB_TILES)
                split2(n + 2)
                steps.begin(i, 1)
                read_tile(kT[:, 0, :], n + 1, t)
                if not is_first:
                    gate_head(i + 8)
                split2(n + 4)
                if is_first:
                    gate_columns()
                dve.wait_ge(ktr_done, i + 1)
                if not is_first:
                    dve.wait_ge(k_stored, i * 32)
                nc.vector.tensor_copy(k_tok[:, :], M[:, 0:(NB + 1) * P]).then_inc(ktok_ready, 1)
                read_tile(qT[:, 0, :], n + 3, t + 1, DH ** -0.5)
                split2(n + 6)
                dve.wait_ge(z_done, i + 1)
                nc.vector.tensor_copy(XA[:, :], M[:, 0:SB_W]).then_inc(zs_ready, 1)
                read_tile(vT[:, 0, :], n + 5, t + 2)
                dve.wait_ge(soft_ready, i + 1)
                nc.vector.scalar_tensor_tensor(XC[:, :], XA[:, :], 0.0, XB[:, :], ALU.max, ALU.add).then_inc(L_ready, 1)
                split2(n + 8)
                dve.wait_ge(xchi_ready, i + 1)
                nc.vector.tensor_tensor(XC_lo[:, :], XC[:, :], XC_hi[:, :].bitcast(F32), ALU.subtract).then_inc(xclo_ready, 1)
                silu_tile(silu[:, 0, :], t + 3, i + 9)
                dve.wait_ge(after_done, i + 1)
                if not is_first:
                    dve.wait_ge(v_stored, i * 32)
                nc.vector.tensor_copy(v_tok[:, :], M[:, SB_W:SB_W + NB * P]).then_inc(vtok_ready, 1)
                steps.link(nc.vector.tensor_tensor(XA[:, :], M[:, 0:SB_W], XA[:, :], ALU.add))
                nc.vector.tensor_scalar(XA[:, :], XA[:, :], 0.0, None, ALU.min).then_inc(s_ready, 1)

            def gate_columns():
                dve.wait_ge(gate_pe, 1)
                nc.vector.tensor_copy(acol[:, :, :].rearrange("p j h -> p (j h)"), M[:, 0:NB * MLH]).then_inc(gate_dve, 1)
                dve.wait_ge(gate_dve, 3)
                dve.wait_ge(gate_loads, 16 * GATE_LOADS)
                nc.vector.tensor_scalar(EM[:, :, :], EM[:, :, :], -EM_MAX, None, ALU.max)
                for h in range(MLH):
                    for lo, hi, tl in ((0, NT, TP - 1), (NT, NB, T - 1)):
                        nc.vector.tensor_scalar(wend[:, h, lo:hi], acol[:, lo:hi, h], G[:, h, tl:tl + 1], 0.0,
                                                ALU.subtract, ALU.min)
                    nc.vector.tensor_scalar(decay[:, h:h + 1], m0b[:, h:h + 1], G[:, h, T - 1:T], None, ALU.subtract)
                    i = nc.vector.tensor_scalar(wi[:, h, :], G[:, h, TP:T], m0b[:, h:h + 1], None, ALU.subtract)
                i.then_inc(gate_dve, 1)

            dve.wait_ge(urow_stored, 32 * POOL_IT)
            head(0, True)
            with dve.Fori(1, SB_IT) as i:
                head(i, False)
            steps.end(SB_IT)
            split2(At(H_ML + 2))
            read_tile(qT[:, 0, :], At(H_ML + 1), At(T_ML))
            gate_head(16)
            dve.wait_ge(k_stored, 32 * SB_IT)
            dve.wait_ge(v_stored, 32 * SB_IT)
            dve.wait_ge(gate_act, 5)
            steps.begin(0, 3)
            steps.link(nc.vector.memset(wend[0:TS, :, NT:NB], 0.0))
            steps.link(nc.vector.tensor_scalar(wend[:, :, :], wend[:, :, :], MDH ** -0.5, None, ALU.mult))
            nc.vector.tensor_copy(ones_r[:, :], ones[:, :])
            two_ones = ones[:, 0:2 * NB].rearrange("p (j c) -> p j c", j=NB)
            nc.vector.tensor_copy(mv_hi[:, :, MDH:MDH + 2], two_ones)
            steps.link(nc.vector.tensor_scalar(mv_lo[:, :, MDH:MDH + 2], two_ones, 0.0, None, ALU.mult))
            steps.end(1)

            def ml_head(i, is_first):
                n, t = At(H_ML, i, ML_HALVES), At(T_ML, i, ML_TILES)
                steps.begin(i, 7)
                if not is_first:
                    read_tile(qT[:, 0, :], n + 1, t)
                split2(n + 4)
                for kb, col, w, q0 in ML_BLOCKS:
                    last = nc.vector.tensor_scalar(XA[:, col:col + w], G[:, bass.ds(i, 1), q0:q0 + w],
                                                   acol[:, kb, bass.ds(i, 1)], 0.0, ALU.subtract, ALU.max)
                last.then_inc(D_ready, 1)
                read_tile(qT[:, 1, :], n + 3, t + 1)
                split2(n + 6)
                read_tile(kT[:, 0, :], n + 5, t + 2)
                split2(n + 8)
                read_tile(kT[:, 1, :], n + 7, t + 3)
                split2(n + 10)
                read_tile(vT[:, 0, :], n + 9, t + 4)
                dve.wait_ge(mktr_done, i + 1)
                dve.wait_ge(mkhi_ready, i + 1)
                for kb in range(NB):
                    last = nc.vector.scalar_tensor_tensor(mk_lo[:, kb, :], M[:, MDH * kb:MDH * (kb + 1)],
                                                          wend[:, bass.ds(i, 1), kb], mk_hi[:, kb, :].bitcast(F32),
                                                          ALU.mult, ALU.subtract)
                last.then_inc(kw_ready, 1)
                split2(n + 12)
                read_tile(vT[:, 1, :], n + 11, t + 5)
                dve.wait_ge(scores_done, i + 1)
                dve.wait_ge(Wm_ready, i + 1)
                nc.vector.scalar_tensor_tensor(XA[:, 0:ML_W], M[:, 0:ML_W], MDH ** -0.5, XA[:, 0:ML_W], ALU.mult, ALU.mult
                                               ).then_inc(sw_ready, 1)
                split2(n + 14)
                dve.wait_ge(shi_ready, i + 1)
                nc.vector.tensor_tensor(S_lo[:, :], XA[:, 0:ML_W], S_hi[:, :].bitcast(F32), ALU.subtract).then_inc(slo_ready, 1)
                dve.wait_ge(mvtr_done, i + 1)
                for c in range(MC):
                    nc.vector.tensor_tensor(qw[:, c, :], qT[:, c, TP:T], wi[:, bass.ds(i, 1), :], ALU.mult)
                    nc.vector.tensor_scalar(n0b[:, c, :], ones[:, :], n0[:, bass.ds(i * MC + c, 1)], None, ALU.mult)
                dve.wait_ge(mvhi_ready, i + 1)
                nc.vector.tensor_tensor(mv_lo[:, :, 0:MDH], M[:, 0:NB * MDH].rearrange("p (j d) -> p j d", j=NB),
                                        mv_hi[:, :, 0:MDH].bitcast(F32), ALU.subtract).then_inc(mvtok_ready, 1)
                split2(n + 16)
                dve.wait_ge(num_done, i + 1)
                dve.wait_ge(states_out, i + 1)
                nc.vector.tensor_copy(num[:, :, 0:TP], M[:, 0:2 * TP].rearrange("p (c t) -> p c t", c=MC))
                nc.vector.tensor_copy(num[:, :, TP:T], M[:, 1536:1536 + MC * TS].rearrange("p (c t) -> p c t", c=MC))
                nc.vector.tensor_copy(den[:, 0:TP], M[:, 1024:1536])
                nc.vector.tensor_copy(den[:, TP:T], M[:, 1536 + MC * TS:1536 + (MC + 1) * TS]).then_inc(num_ready, 1)
                split2(n + 18)
                dve.wait_ge(dabs_ready, i + 1)
                nc.vector.scalar_tensor_tensor(den, den, DEN_MIN, EM[:, bass.ds(i, 1), :].rearrange("p a t -> p (a t)"),
                                               ALU.max, ALU.max).then_inc(dmax_ready, 1)
                silu_tile(silu[:, 0, :], t + 8, i * 2 + 17)
                evacuated(dve, t + 8)
                steps.link(nc.vector.tensor_tensor(silu[:, 0, :], silu[:, 0, :], og[:, 0, :], ALU.mult))
                dve.wait_ge(ssq_done, i + 1)
                dve.wait_ge(dsq_ready, i + 1)
                nc.vector.scalar_tensor_tensor(two(den), M[:, 0:1024].rearrange("p (b t) -> p b t", b=2)[:, :, 0:TH],
                                               1.0 / MDH, two(den), ALU.mult, ALU.add).then_inc(ssq_read, 1)
                split2(n + 20)
                dve.wait_ge(root_ready, i + 1)
                steps.link(nc.vector.reciprocal(den, den))
                silu_tile(silu[:, 1, :], t + 9, i * 2 + 18)
                evacuated(dve, t + 9)
                steps.link(nc.vector.tensor_tensor(silu[:, 1, :], silu[:, 1, :], og[:, 1, :], ALU.mult))
                for c in range(MC):
                    steps.link(nc.vector.tensor_tensor(num[:, c, :], num[:, c, :], den, ALU.mult))
                    nc.vector.scalar_tensor_tensor(gated[:, :], num[:, c, :], hnorm[:, bass.ds(i * MC + c, 1)],
                                                   silu[:, c, :], ALU.mult, ALU.mult).then_inc(g_ready, 1)
                    gated_lo(i * 2 + (17 + c))
                    if c == 0:
                        split2(n + 22)
                dve.wait_ge(state_done, i + 1)
                new = M[:, :].rearrange("p (s c v) -> p s c v", s=2, c=MC)
                nc.vector.tensor_copy(states[:, 0:MC * MDH].rearrange("p (c v) -> p c v", c=MC), new[:, 0, :, 0:MDH])
                nc.vector.tensor_copy(n_out[:, 0, bass.ds(i * MC, MC)], new[:, 0, :, MDH:MDH + 1].rearrange("p c v -> p (c v)"))
                steps.link(nc.vector.tensor_scalar(n_decayed[:, :], n0[:, bass.ds(i * MC, MC)], decay[:, bass.ds(i, 1)], None, ALU.mult))
                steps.link(nc.vector.tensor_tensor(n_out[:, 1, bass.ds(i * MC, MC)], new[:, 1, :, MDH:MDH + 1].rearrange("p c v -> p (c v)"),
                                                   n_decayed[:, :], ALU.add))
                nc.vector.scalar_tensor_tensor(states[:, MC * MDH:2 * MC * MDH].rearrange("p (c v) -> p c v", c=MC), c0[:, :, :],
                                               decay[:, bass.ds(i, 1)], new[:, 1, :, 0:MDH], ALU.mult, ALU.add
                                               ).then_inc(state_ready, 1)

            ml_head(0, True)
            with dve.Fori(1, ML_IT) as i:
                ml_head(i, False)
            steps.end(ML_IT)

            def merge_tiles(it, dd, opens, is_first=False, is_last=False):
                n, t = At(H_MG, it, MG_HALVES), At(T_MG, it, MG_TILES)
                for j in (0, 2):
                    for s in (2, 4, 6):
                        if not (is_first and j == 0 and s == 2):
                            split2(n + (3 * j + s))
                    for c in range(2):
                        if is_last and j == 2:
                            merged_lo(*((0, KD // 2 + 1), (KD // 2 + 1, KD - 2))[c])
                        evacuated(dve, t + (2 * j + c))
                        dve.wait_ge(w_used, (n + (3 * j + 4 + c)).value(1))
                        if is_first and j == 0 and c == 0:
                            dve.wait_ge(merged_free, 1)
                        m = merged[:, bass.ds(dd * 4 + (j + c), 1), :].rearrange("p a t -> p (a t)")
                        i = nc.vector.tensor_tensor(two(m if opens else term[:, c, :]), pair(t + (2 * j + 2 + c)),
                                                    two(gsig[:, c, :]), ALU.mult)
                        i.then_inc(psum_free[(t + c).base % 2], 1)
                        if not opens:
                            evacuated(dve, t + (2 * j + 2 + c))
                            nc.vector.tensor_tensor(m, m, term[:, c, :], ALU.add).then_inc(branch_done, 1)

            def merged_lo(k0, k1):
                for k in range(k0, k1):
                    dve.wait_ge(mhi_ready, k + 1)
                    nc.vector.tensor_tensor(x_lo[:, k, :], merged[:, k, :], x_hi[:, k, :].bitcast(F32), ALU.subtract
                                            ).then_inc(mlo_ready, 1)

            merge_tiles(0, 0, True, is_first=True)
            with dve.Fori(1, 4) as dd:
                merge_tiles(dd, dd, True)
            with dve.Fori(0, 4) as dd:
                merge_tiles(dd + 4, dd, False)
            with dve.Fori(0, 3) as dd:
                merge_tiles(dd + 4 * (NBR - 1), dd, False)
            merge_tiles(MG_IT - 1, 3, False, is_last=True)
            merged_lo(KD - 2, KD)
            dve.wait_ge(mlo_ready, KD)
            steps.begin(0, 1)
            steps.link(nc.vector.memset(ysums[:, :, :], 1.0))
            steps.end(1)

            def read_y(nr):
                if not (isinstance(nr.i, int) and nr.base == 0):
                    dve.wait_ge(ytr_done, nr.value())
                read_tile(yT[:, :], At(H_OUT + 2 * nr.base + 1, nr.i, 2 * nr.per), At(T_OUT + nr.base, nr.i, nr.per))

            def scale_y(nr):
                dve.wait_ge(ytr_done, nr.value(1))
                for m in range(NB):
                    rows = P if m < NT else TS
                    at = 1024 * (nr.base % 2) + P * m
                    cols = bass.ds(nr.value() * P, P)
                    last = nc.vector.tensor_tensor(y_tok[0:rows, m, cols], M[0:rows, at:at + P], gpost_b[0:rows, cols],
                                                   ALU.mult)
                last.then_inc(yg_ready, 1)

            split2(At(H_OUT + 2))
            read_y(At(0))
            split2(At(H_OUT + 4))
            dve.wait_ge(gain_y_loaded, 16)
            scale_y(At(0))
            read_y(At(1))
            with dve.Fori(0, OUT_IT - 2) as d:
                n, nr = At(H_OUT + 6, d, OUT_HALVES), At(1, d, OUT_TILES)
                for j in range(2):
                    split2(n + 2 * j)
                    scale_y(nr + j)
                    read_y(nr + (j + 1))
            split2(At(H_OUT + 2 * KD - 2))
            for nr in range(KD - 3, KD):
                scale_y(At(nr))
                if nr < KD - 1:
                    read_y(At(nr + 1))
            dve.wait_ge(ysq_done, KD)
            steps.begin(0, 2)
            steps.link(nc.vector.tensor_reduce(ss_y, ysums[:, :, :], AXX, ALU.add))
            nc.vector.tensor_scalar(ss_y, ss_y, 1.0 / D, EPS, ALU.mult, ALU.add).then_inc(yms_ready, 1)
            dve.wait_ge(root_y_ready, 1)
            dve.wait_ge(x_again_loaded, 32)
            steps.link(nc.vector.reciprocal(rs_y, rs_y))
            steps.end(1)
            for m in range(NB):
                rows = P if m < NT else TS
                nc.vector.scalar_tensor_tensor(y_tok[0:rows, m, :], y_tok[0:rows, m, :], rs_y[0:rows, m:m + 1],
                                               x_again[0:rows, m, :], ALU.mult, ALU.add).then_inc(yout_ready, 1)

        @block.gpsimd
        def _(pool):
            steps = Steps(pool, pool_steps)

            def own_wait():
                pool.sem_inc(pool_turns, 1)

            pool.sem_inc(states_out, 1)
            vectors = [(hnorm[:, :], ml_hnorm.rearrange("a (k p) -> p (a k)", p=P)),
                       (pscale[:, :], pool_scale.rearrange("a (k p) -> p (a k)", p=P)),
                       (bif, b_if.rearrange("a r h -> (r h) a")),
                       (m0row, state_ml_m.rearrange("a b h -> h (a b)"))]
            assert len(vectors) == VECTORS
            for dst, src in vectors:
                pool.dma_start(dst, src, allow_slow_non_contiguous=True).then_inc(vectors_loaded, 16)
            steps.begin(0, 2)
            steps.link(nc.gpsimd.memset(ident[:, :], 0.0))
            nc.gpsimd.affine_select(ident[:, :], ident[:, :], pattern=[[-1, P]], compare_op=ALU.not_equal, fill=1.0,
                                    base=0, channel_multiplier=1).then_inc(consts_ready, 1)
            nc.gpsimd.memset(ones[:, :], 1.0).then_inc(consts_ready, 1)
            nc.gpsimd.memset(negones_f[:, :], -1.0).then_inc(consts_ready, 1)
            steps.link(nc.gpsimd.memset(negtri_f[:, :], -1.0))
            nc.gpsimd.affine_select(negtri_f[:, :], negtri_f[:, :], pattern=[[-1, P]], compare_op=ALU.is_ge, fill=0.0,
                                    base=0, channel_multiplier=1).then_inc(consts_ready, 1)
            steps.end(1)

            def build_mask(strict):
                steps.begin(0, 1 + len(MASK_KEYS) + 1)
                steps.link(nc.gpsimd.memset(mask[:, :], 1.0))
                for j, kb in enumerate(MASK_KEYS):
                    c, w = (j * P, P) if kb < NT else (j * P, TS)
                    steps.link(nc.gpsimd.affine_select(mask[:, c:c + w], mask[:, c:c + w], pattern=[[1, w]],
                                                       compare_op=ALU.is_gt if strict else ALU.is_ge, fill=0.0,
                                                       base=0 if kb < NT else TS, channel_multiplier=-1))
                steps.link(nc.gpsimd.affine_select(mask[:, c:c + w], mask[:, c:c + w], pattern=[[0, w]],
                                                   compare_op=ALU.is_ge, fill=0.0, base=-TS, channel_multiplier=1))
                steps.end(1)

            def apply_mask(X, masked):
                for col, c, w in masked:
                    i = nc.gpsimd.tensor_tensor(X[:, col:col + w], X[:, col:col + w], mask[:, c:c + w], ALU.mult)
                return i

            def store_gated(k, tile_nr):
                pool.wait_ge(glo_ready, k)
                for s, src in enumerate((g_hi, g_lo)):
                    pool.dma_start(gated_v[:, s, bass.ds(tile_nr, 1), :].rearrange("p a t -> p (a t)"), src[:, :]
                                   ).then_inc(g_stored, 16)

            pool.wait_ge(gain_loaded, 16)
            for m in POOLS_BLOCKS:
                rows = P if m < NT else TS
                pool.wait_ge(sq_done, m + 1)
                nc.gpsimd.tensor_tensor(xt[0:rows, m, :], xt[0:rows, m, :], gpre_b[0:rows, :], ALU.mult
                                        ).then_inc(xg_ready, 1)
            pool.wait_ge(xlo_done, 4 * NB)
            pool.dma_start(spool[:, :], state_pool[0, 0, :, :]).then_inc(spool_loaded, 16)
            def load_wp(g):
                pool.wait_ge(wpool_done, g + 1)
                pool.dma_start(wp[:, :, :, :], w_pool_v[:, bass.ds(g, 1), :, :]).then_inc(wp_loaded, 16)

            load_wp(0)
            pool.dma_start(m0b[:, :], state_ml_m[0, 0, :].partition_broadcast(P)).then_inc(gate_loads, 16)
            pool.dma_start(n0[:, :], n0_v, allow_slow_non_contiguous=True).then_inc(gate_loads, 16)
            pool.wait_ge(gate_dve, 1)
            pool.dma_start(fsel[:, :], lf[MLH:ROWS, :]).then_inc(fsel_loaded, 16)
            pool.wait_ge(gate_dve, 2)
            for s, row in enumerate((grow, frow)):
                pool.dma_start(rows_dram[s, :].rearrange("(h t) -> h t", h=MLH), row[:, :]).then_inc(rows_stored, 16)
            pool.dma_start(p_m.rearrange("a b h -> h (a b)"), frow[:, TP - 1:TP], allow_slow_non_contiguous=True).then_inc(m_stored, 16)
            pool.dma_start(s_m.rearrange("a b h -> h (a b)"), frow[:, T - 1:T], allow_slow_non_contiguous=True).then_inc(m_stored, 16)
            pool.wait_ge(rows_stored, 32)
            for s, dst in enumerate((G, EM)):
                pool.dma_start(dst[:, :, :].rearrange("p h t -> p (h t)"), rows_dram[s, :].partition_broadcast(P)
                               ).then_inc(gate_loads, 16)
            pool.wait_ge(m_stored, 32)

            def group(g, is_first):
                if not is_first:
                    load_wp(g)
                store_gated(g * 2 + 1, g * 2)
                store_gated(g * 2 + 2, g * 2 + 1)
                pool.wait_ge(urow_copied, g + 2)
                rows = pool_row[:, :].rearrange("t (c s d) -> t c s d", c=2, s=2)
                for s, dst in enumerate((p_pool_v, s_pool_v)):
                    pool.dma_start(dst[:, bass.ds(g * (2 * P), 2 * P)].rearrange("t (c d) -> t c d", c=2), rows[:, :, s, :]
                                   ).then_inc(urow_stored, 16)

            group(0, True)
            with pool.Fori(1, POOL_IT) as g:
                group(g, False)
            pool.wait_ge(urow_stored, 32 * POOL_IT)
            pool.wait_ge(gate_pe, 1)
            build_mask(True)

            def head(i, is_first):
                if not is_first:
                    pool.wait_ge(ktr_done, i * 1)
                pool.dma_start(past_k[:, :], past_k_v[:, bass.ds(i * P, P)]).then_inc(past_k_loaded, 16)
                if not is_first:
                    store_gated(i + 8, i + 7)
                pool.dma_start(past_v[:, :], past_v_v[:, bass.ds(i * P, P)]).then_inc(past_v_loaded, 16)
                pool.wait_ge(ktok_ready, i + 1)
                own_wait()
                pool.dma_start(pk_v[:, :, bass.ds(i * P, P)], k_tok[:, 0:NT * P].rearrange("p (m d) -> p m d", m=NT)
                               ).then_inc(k_stored, 16)
                pool.dma_start(sk_v[:, bass.ds(i * P, P)], k_tok[TS:P, NT * P:NB * P]).then_inc(k_stored, 16)
                pool.wait_ge(L_ready, i + 1)
                apply_mask(XC, SB_MASKED).then_inc(Lm_ready, 1)
                pool.wait_ge(a_ready, i + 1)
                apply_mask(XB, SB_MASKED).then_inc(am_ready, 1)
                pool.dma_start(pv_v[:, :, bass.ds(i * P, P)], v_tok[:, P:NB * P].rearrange("p (m d) -> p m d", m=NT)
                               ).then_inc(v_stored, 16)
                pool.dma_start(sv_v[:, bass.ds(i * P, P)], v_tok[TS:P, 0:P]).then_inc(v_stored, 16)

            head(0, True)
            with pool.Fori(1, SB_IT) as i:
                head(i, False)
            store_gated(16, 15)

            pool.wait_ge(av_done, SB_IT)
            pool.wait_ge(k_stored, 32 * SB_IT)
            pool.wait_ge(v_stored, 32 * SB_IT)
            build_mask(False)
            def load_gated(s, b):
                pool.dma_start((gt_hi, gt_lo)[s][:, :, :], gated_v[:, s, bass.ds(b * KW, KW), :]).then_inc(gt_loaded, 16)

            def ml_head(i, is_last):
                pool.wait_ge(state_ready, i + 1)
                pool.dma_start(c0[:, :, :], c0_v[:, i, :, :]).then_inc(c0_loaded, 16)
                pool.wait_ge(W_ready, i + 1)
                apply_mask(XA, ML_MASKED).then_inc(Wm_ready, 1)
                if is_last:
                    pool.wait_ge(g_stored, 32 * KW)
                    pool.wait_ge(dmax_ready, MLH)
                    load_gated(0, 0)
                store_gated(i * 2 + 17, i * 2 + 16)
                store_gated(i * 2 + 18, i * 2 + 17)
                if is_last:
                    load_gated(1, 0)
                pool.wait_ge(state_ready, i + 2)
                own_wait()
                for s, dst in enumerate((p_c_v, s_c_v)):
                    pool.dma_start(dst[:, i, :, :], states[:, s * MC * MDH:(s + 1) * MC * MDH].rearrange("p (c v) -> p c v", c=MC)
                                   ).then_inc(state_stored, 16)
                if not is_last:
                    pool.wait_ge(state_stored, i * 32 + 32)
                    pool.sem_inc(states_out, 1)

            with pool.Fori(0, ML_IT - 1) as i:
                ml_head(i, False)
            ml_head(ML_IT - 1, True)
            pool.dma_start(p_n_v, n_out[:, 0, :], allow_slow_non_contiguous=True).then_inc(n_stored, 16)
            pool.dma_start(s_n_v, n_out[:, 1, :], allow_slow_non_contiguous=True).then_inc(n_stored, 16)
            pool.wait_ge(n_stored, 32)
            pool.wait_ge(state_stored, 32 * ML_IT)
            pool.sem_inc(merged_free, 1)
            pool.wait_ge(g_stored, 32 * NBR * KW)
            with pool.Fori(1, NBR) as b:
                pool.wait_ge(w_used, b * (4 * MG_HALVES) + H_MG)
                for s in range(2):
                    load_gated(s, b)
            pool.wait_ge(mlo_ready, KD)
            pool.dma_start(gpost_b[:, :], g_post[0, :].partition_broadcast(P)).then_inc(gain_y_loaded, 16)
            pool.dma_start(x_again[:, 0:NT, :], xp_v).then_inc(x_again_loaded, 16)
            pool.dma_start(x_again[0:TS, NT, :], x_sample[0, :, :]).then_inc(x_again_loaded, 16)


_INS = ["x_prompt", "x_sample", "cache_sb_k", "cache_sb_v", "state_pool", "state_ml_c", "state_ml_n", "state_ml_m",
        "g_pre", "w_in", "b_if", "w_pool", "pool_scale", "ml_hnorm", "w_branch", "w_out", "g_post"]
_OUTS = [(1, TP, D), (1, TS, D), (1, 1, TP, SBH, DH), (1, 1, TP, SBH, DH), (1, 1, PST, W), (1, 1, MLH, MDH, MDH),
         (1, 1, MLH, MDH), (1, 1, MLH), (1, 1, TS, SBH, DH), (1, 1, TS, SBH, DH), (1, 1, PST, W),
         (1, 1, MLH, MDH, MDH), (1, 1, MLH, MDH), (1, 1, MLH)]


def kernel(**inputs):
    import numpy as _np
    import concourse.bacc as _bacc
    from concourse import mybir as _mybir
    from concourse.bass_utils import run_bass_kernel_spmd as _run

    nc = _bacc.Bacc("TRN2", target_bir_lowering=False, num_devices=1)
    arrays, args = {}, []
    for name in _INS:
        a = _np.ascontiguousarray(inputs[name])
        arrays[f"in_{name}_dram"] = a
        args.append(nc.dram_tensor(f"in_{name}_dram", a.shape, _mybir.dt.from_np(a.dtype), kind="ExternalInput").ap())
    for i, shape in enumerate(_OUTS):
        args.append(nc.dram_tensor(f"out_{i}_dram", shape, _mybir.dt.float32, kind="ExternalOutput").ap())
    hybrid_layer(nc, *args)
    r = _run(nc, [arrays], core_ids=[0])
    return tuple(r.results[0][f"out_{i}_dram"] for i in range(len(_OUTS)))
```
